# Optimizing a Trainium2 kernel written in Bass

```python
import math
import jax, jax.numpy as jnp
from jax import lax
import numpy as np

D_MODEL = 1024
BATCH = 1
SEQ = 1024
DEPTH = 1

N_POOL_GROUPS = 4
POOL_WINDOWS = (2, 4, 8, 16)
D_POOL = D_MODEL // 2
POOL_GROUP_DIM = D_POOL // N_POOL_GROUPS
HEAD_DIM = 64
D_ATTN = D_MODEL - D_POOL
N_HEADS = D_ATTN // HEAD_DIM
D_MIX = D_POOL + D_ATTN
D_IN = D_POOL + 3 * D_ATTN
D_FF = ((8 * D_MODEL // 3 + 255) // 256) * 256
CONV_WIDTH = 3
Q_BLOCK = 128
N_MOD = 6
EPS = 1e-6

kernel_name = "hybrid_pool_stickbreaking_convffn_adaln"

def rmsnorm(x, g):
    xf = x.astype(jnp.float32)
    y = xf * lax.rsqrt(jnp.mean(xf * xf, axis=-1, keepdims=True) + EPS)
    return (y * g.astype(jnp.float32)).astype(x.dtype)

def modulate(h, shift, scale):
    return h * (1.0 + scale[:, None, :]) + shift[:, None, :]

def pool_mixer(u, pool_w, pool_b, pool_scale):
    b, s, _ = u.shape
    uf = u.astype(jnp.float32).reshape(b, s, N_POOL_GROUPS, POOL_GROUP_DIM)
    cs = jnp.concatenate([jnp.zeros_like(uf[:, :1]), jnp.cumsum(uf, axis=1)], axis=1)
    t1 = jnp.arange(1, s + 1)
    outs = []
    for g, w in enumerate(POOL_WINDOWS):
        cg = cs[:, :, g]
        lo = jnp.maximum(t1 - w, 0)
        win_sum = cg[:, 1:] - cg[:, lo]
        count = jnp.minimum(t1, w).astype(jnp.float32)
        outs.append(win_sum / count[None, :, None] - uf[:, :, g])
    pooled = jnp.stack(outs, axis=2)
    y = jnp.einsum('bsgc,gcd->bsgd', pooled, pool_w.astype(jnp.float32)) + pool_b.astype(jnp.float32)
    y = y.reshape(b, s, D_POOL) * pool_scale.astype(jnp.float32)
    return y.astype(u.dtype)

def stick_breaking_attention(q, k, v):
    b, h, s, d = q.shape
    nb = s // Q_BLOCK
    qb = q.reshape(b, h, nb, Q_BLOCK, d).transpose(2, 0, 1, 3, 4)
    k_pos = jnp.arange(s)
    inv_sqrt_d = 1.0 / math.sqrt(d)

    def one_block(args):
        q_blk, blk = args
        q_pos = blk * Q_BLOCK + jnp.arange(Q_BLOCK)
        causal = k_pos[None, :] < q_pos[:, None]
        z = jnp.einsum('bhqd,bhkd->bhqk', q_blk, k) * inv_sqrt_d
        log_beta = jax.nn.log_sigmoid(z)
        log_1m = jnp.where(causal, jax.nn.log_sigmoid(-z), 0.0)
        later = lax.cumsum(log_1m, axis=3, reverse=True) - log_1m
        a = jnp.exp(jnp.where(causal, log_beta + later, -jnp.inf))
        return jnp.einsum('bhqk,bhkd->bhqd', a, v)

    o = lax.map(one_block, (qb, jnp.arange(nb)))
    return o.transpose(1, 2, 0, 3, 4).reshape(b, h, s, d)

def causal_depthwise_conv(u, w, bias):
    ch = u.shape[-1]
    y = lax.conv_general_dilated(
        u, w[:, None, :].astype(u.dtype), window_strides=(1,),
        padding=[(CONV_WIDTH - 1, 0)], dimension_numbers=('NWC', 'WIO', 'NWC'),
        feature_group_count=ch)
    return y + bias.astype(u.dtype)

def setup_inputs(seed: int = 0) -> dict:
    key = jax.random.key(seed)
    ks = jax.random.split(key, 20)
    f32 = jnp.float32
    n = lambda k, shape, s: jax.random.normal(k, shape, f32) * s
    return {
        "x": n(ks[0], (BATCH, SEQ, D_MODEL), 1.0),
        "c": n(ks[1], (BATCH, D_MODEL), 1.0),
        "ada_w": n(ks[2], (DEPTH, D_MODEL, N_MOD * D_MODEL), 0.5 * D_MODEL ** -0.5),
        "ada_b": n(ks[3], (DEPTH, N_MOD * D_MODEL), 0.02),
        "norm1_g": 1.0 + n(ks[4], (DEPTH, D_MODEL), 0.05),
        "w_in": n(ks[5], (DEPTH, D_MODEL, D_IN), D_MODEL ** -0.5),
        "pool_w": n(ks[6], (DEPTH, N_POOL_GROUPS, POOL_GROUP_DIM, POOL_GROUP_DIM), POOL_GROUP_DIM ** -0.5),
        "pool_b": n(ks[7], (DEPTH, N_POOL_GROUPS, POOL_GROUP_DIM), 0.02),
        "pool_scale": 1.0 + n(ks[8], (DEPTH, D_POOL), 0.1),
        "q_norm_g": 1.0 + n(ks[9], (DEPTH, HEAD_DIM), 0.05),
        "k_norm_g": 1.0 + n(ks[10], (DEPTH, HEAD_DIM), 0.05),
        "attn_out_g": 1.0 + n(ks[11], (DEPTH, N_HEADS, HEAD_DIM), 0.05),
        "w_out": n(ks[12], (DEPTH, D_MIX, D_MODEL), D_MIX ** -0.5),
        "norm2_g": 1.0 + n(ks[13], (DEPTH, D_MODEL), 0.05),
        "w_up": n(ks[14], (DEPTH, D_MODEL, 2 * D_FF), D_MODEL ** -0.5),
        "conv_w": n(ks[15], (DEPTH, CONV_WIDTH, 2 * D_FF), CONV_WIDTH ** -0.5),
        "conv_b": n(ks[16], (DEPTH, 2 * D_FF), 0.02),
        "w_down": n(ks[17], (DEPTH, D_FF, D_MODEL), D_FF ** -0.5),
    }

def reference(x, c, ada_w, ada_b, norm1_g, w_in, pool_w, pool_b, pool_scale, q_norm_g, k_norm_g,
              attn_out_g, w_out, norm2_g, w_up, conv_w, conv_b, w_down):
    b, s, _ = x.shape
    c_act = jax.nn.silu(c)
    for l in range(DEPTH):
        mod = jnp.einsum('bd,de->be', c_act, ada_w[l]) + ada_b[l]
        shift1, scale1, gate1, shift2, scale2, gate2 = jnp.split(mod, N_MOD, axis=-1)

        h = modulate(rmsnorm(x, norm1_g[l]), shift1, scale1)
        proj = jnp.einsum('bsd,de->bse', h, w_in[l])
        u, q, k, v = jnp.split(proj, [D_POOL, D_POOL + D_ATTN, D_POOL + 2 * D_ATTN], axis=-1)

        y_pool = pool_mixer(u, pool_w[l], pool_b[l], pool_scale[l])

        to_heads = lambda t: t.reshape(b, s, N_HEADS, HEAD_DIM).transpose(0, 2, 1, 3)
        qh = rmsnorm(to_heads(q), q_norm_g[l]).astype(jnp.float32)
        kh = rmsnorm(to_heads(k), k_norm_g[l]).astype(jnp.float32)
        vh = to_heads(v).astype(jnp.float32)
        o = stick_breaking_attention(qh, kh, vh)
        o = o.transpose(0, 2, 1, 3).astype(x.dtype)
        o = rmsnorm(o, attn_out_g[l]).reshape(b, s, D_ATTN)

        mix = jnp.concatenate([y_pool, o], axis=-1)
        x = x + gate1[:, None, :] * jnp.einsum('bse,ed->bsd', mix, w_out[l])

        h2 = modulate(rmsnorm(x, norm2_g[l]), shift2, scale2)
        up = jnp.einsum('bsd,df->bsf', h2, w_up[l])
        up = causal_depthwise_conv(up, conv_w[l], conv_b[l])
        gate, val = jnp.split(up, 2, axis=-1)
        ffn = jnp.einsum('bsf,fd->bsd', jax.nn.silu(gate) * val, w_down[l])
        x = x + gate2[:, None, :] * ffn
    return x


_drawn_inputs = setup_inputs


def setup_inputs(seed=0):
    import zlib

    import numpy as np

    out = dict(_drawn_inputs(seed))
    spreads = {}
    factors = {'norm1_g': 3.821,
     'pool_b': 8.0,
     'pool_scale': 3.098,
     'q_norm_g': 8.0,
     'k_norm_g': 8.0,
     'attn_out_g': 5.294,
     'norm2_g': 3.852,
     'conv_b': 8.0}
    for name, (base, spread) in spreads.items():
        noise = np.random.default_rng([zlib.crc32(name.encode()), seed]).standard_normal(out[name].shape)
        drawn = base * np.exp(spread * noise) if base else spread * noise
        out[name] = __import__('jax').numpy.asarray(drawn.astype(out[name].dtype))
    for name, factor in factors.items():
        out[name] = (out[name] * factor).astype(out[name].dtype)
    return out
```

```python
from contextlib import ExitStack

import concourse.bass as bass
from concourse import mybir

F32 = mybir.dt.float32
F32R = mybir.dt.float32r
BF16 = mybir.dt.bfloat16
U32 = mybir.dt.uint32
ALU = mybir.AluOpType
ACT = mybir.ActivationFunctionType
ds = bass.ds

P = 128
HALF = 512
EPS = 1e-6
POOL_WINDOWS = (2, 4, 8, 16)
PAD = max(POOL_WINDOWS)
MASKED = -1e30
ABS_BITS = 0x7FFFFFFF

C_IDENT, C_TRI, C_HEADAVG, C_RAMP, C_MASK, C_END = 0, 128, 256, 384, 400, 528


def shape_constants():
    import numpy as np
    c = np.zeros((P, C_END), np.float32)
    r = np.arange(P)
    c[:, C_IDENT:C_TRI] = np.eye(P)
    c[:, C_TRI:C_HEADAVG] = np.where(r[:, None] >= r[None, :], -1.0, 0.0)
    c[:, C_HEADAVG:C_RAMP] = (r[:, None] // 64 == r[None, :] // 64) / 64.0
    c[:, C_RAMP:C_MASK] = PAD / (np.arange(PAD) + 1.0)
    c[:, C_MASK:C_END] = np.where(r[:, None] >= r[None, :], MASKED, 0.0)
    return c


def hybrid_layer(nc, x, c, ada_w, ada_b, norm1_g, w_in, pool_w, pool_b, pool_scale, q_norm_g,
                 k_norm_g, attn_out_g, w_out, norm2_g, w_up, conv_w, conv_b, w_down, consts, out):
    S, D = x.shape[1], x.shape[2]
    KT = D // P
    DP = pool_w.shape[1] * pool_w.shape[2]
    GROUPS = pool_w.shape[1]
    D_IN = w_in.shape[2]
    DFF = w_down.shape[1]
    FT = DFF // P
    NG = FT // 2
    NPAIR = (D - DP) // P
    N_IN = D_IN // P
    T_OUT, T_UP = N_IN, N_IN + KT
    T_Q, T_K, T_V = DP // P, DP // P + NPAIR, DP // P + 2 * NPAIR
    SB = S // P
    assert S == 2 * HALF and KT == 8 and NPAIR == 4 and GROUPS == 4 and FT % 2 == 0

    UNITS = [(par, h, i) for par in range(2) for h in range(2) for i in range(4 * h + 3, -1, -1)]
    NU = len(UNITS)
    BODY = UNITS + UNITS
    NB = len(BODY)
    SEQ_OF = [sum(1 for u in BODY[:n + 1] if u[2] == 4 * u[1] + 3) - 1 for n in range(NB)]
    ADDS_BEFORE = [sum(1 for u in BODY[:n] if u[2] > 0) for n in range(NB + 1)]
    NSEQ = SEQ_OF[-1] + 1
    LAST_OF = [max(n for n in range(NB) if SEQ_OF[n] == s) for s in range(NSEQ)]

    def col0(n):
        par, h, i = BODY[n]
        return max(0, P * i - HALF * h)

    with ExitStack() as ctx:
        BASE = (nc.sbuf_base + 31) // 32 * 32
        KB = 1024
        X0 = BASE
        R1 = X0 + 32 * KB
        KQ0 = R1 + 64 * KB
        V0 = KQ0 + 32 * KB
        PB0 = V0 + 16 * KB
        W0 = PB0 + 32 * KB + 256
        C0 = W0 + 24 * KB
        place = [C0]

        def at(name, shape, dt, off):
            return nc.alloc_sbuf_tensor_at(name, shape, dt, offset=off)

        def small(name, cols, dt=F32):
            t = at(name, [P, cols], dt, place[0])
            place[0] += (cols * mybir.dt.size(dt) + 31) // 32 * 32
            return t

        xT = at("xT", [P, KT, S], F32, X0)
        act_hi = at("act_hi", [P, KT, S], F32R, R1)
        act_lo = at("act_lo", [P, KT, S], F32R, R1 + 32 * KB)
        acc_first = [at(f"acc_first{b}", [P, 512], F32, R1 + 8 * KB + 2 * KB * b) for b in range(2)]
        x_tok = at("x_tok", [P, SB, D], F32, R1 + 32 * KB)
        prow = at("param_rows", [P, 3, P], F32, R1)
        kq = at("kq", [P, 2 * NPAIR, S], F32, KQ0)
        kq_f = kq[:, :, :].rearrange("p a b -> p (a b)")
        v_tok = at("v_tok", [P, SB, NPAIR * P], F32, V0)
        ada_at = [KQ0, KQ0 + 8 * KB, KQ0 + 16 * KB, KQ0 + 24 * KB, V0, V0 + 8 * KB, PB0, PB0 + 8 * KB]
        ada_piece = [at(f"ada_piece{s}", [P, KT, 256], F32, o) for s, o in enumerate(ada_at)]
        w_raw = [at(f"w_raw{b}", [P, KT, P], F32, W0 + 4 * KB * b) for b in range(2)]
        w_hi = [at(f"w_hi{b}", [P, KT, P], F32R, W0 + 8 * KB + 4 * KB * b) for b in range(2)]
        w_lo = [at(f"w_lo{b}", [P, KT, P], F32R, W0 + 16 * KB + 4 * KB * b) for b in range(2)]
        ssum = at("ssum", [P, S], F32, PB0 + 16 * KB)
        sqx = [at(f"sqx{b}", [P, HALF], F32, PB0 + 20 * KB + 2 * KB * b) for b in range(2)]
        tnorm = [at(f"tnorm{b}", [P, S], F32, PB0 + 24 * KB + 4 * KB * b) for b in range(2)]
        UP = 4 * (PAD + S)
        u_pad = [at(f"u_pad{g}", [P, PAD + S], F32, W0 - UP * (GROUPS - g)) for g in range(GROUPS)]
        wsum = [at(f"wsum{b}", [P, PAD + S], F32, PB0 + UP * b) for b in range(2)]
        wpool = at("wpool", [P, GROUPS * P], F32, PB0 + 2 * UP + 4 * S)
        hn = [at("hn0", [P, S], F32, PB0 + 2 * UP), at("hn1", [P, S], F32, PB0)]
        names = ("q_hi", "q_lo", "k_hi", "k_lo")
        qh, ql, kh, kl = ([at(f"{n}{b}", [P, S], F32R, PB0 + 16 * KB * b + 4 * KB * j) for b in range(2)]
                          for j, n in enumerate(names))
        T1, T2 = R1 + 16 * KB, R1 + 48 * KB
        soft = [at(f"soft{b}", [P, HALF], F32, T1 + 2 * KB * b) for b in range(3)]
        loss = [at(f"loss{b}", [P, HALF], F32, T1 + 2 * KB * (3 + b)) for b in range(3)]
        later = [at(f"later{b}", [P, HALF], F32, T1 + 2 * KB * (6 + b)) for b in range(2)]
        attn = [at(f"attn{b}", [P, HALF], F32, T2 + 2 * KB * b) for b in range(3)]
        vp = [at(f"v_pair{b}", [P, SB, P], F32, T2 + 8 * KB + 4 * KB * b) for b in range(2)]
        on = [at(f"on{b}", [P, S], F32, PB0 + 4 * KB * b) for b in range(2)]
        osq = [at(f"osq{b}", [P, S], F32, PB0 + 8 * KB + 4 * KB * b) for b in range(NPAIR)]
        sq2 = [at(f"sq2{b}", [P, S], F32, PB0 + 20 * KB + 4 * KB * b) for b in range(2)]
        t2 = [at(f"t2{b}", [P, S], F32, PB0 + 4 * KB * b) for b in range(2)]
        ff_hi = at("ff_hi", [P, 2, S], F32R, KQ0)
        ff_lo = at("ff_lo", [P, 2, S], F32R, KQ0 + 8 * KB)
        wd_hi = at("wd_hi", [P, 2, D], F32R, KQ0 + 16 * KB)
        wd_lo = at("wd_lo", [P, 2, D], F32R, KQ0 + 24 * KB)
        wd_raw = at("wd_raw", [P, 2, D], F32, V0)
        cgate = [at(f"cgate{b}", [P, S], F32, PB0 + 8 * KB + 4 * KB * b) for b in range(2)]
        cval = [at("cval0", [P, S], F32, V0 + 8 * KB), at("cval1", [P, S], F32, V0 + 12 * KB)]
        silu = [at(f"silu{b}", [P, S], F32, PB0 + 16 * KB + 4 * KB * b) for b in range(2)]
        o_sb = [at(f"o_sb{b}", [P, SB, P], F32, PB0 + 24 * KB + 4 * KB * b) for b in range(2)]

        cst = small("cst", C_MASK)
        maskf = at("maskf", [P, P], F32, R1 + 4 * KB)
        negones, ones = small("negones", P), small("ones", P)
        ident_b, mask_b = small("ident_b", P, BF16), small("mask_b", P, BF16)
        acc = small("ada_acc", 512)
        one = small("one", 1)
        c_raw, c_act = small("c_raw", KT), small("c_act", KT)
        NPAR = 48 + 2 * KT + 2 * GROUPS + NPAIR + 2
        pcol = small("pcol", NPAR + 8 * FT)
        modc = small("modc", 48)
        gain = small("gain", 2 * KT)
        qg8 = small("qg8", 1)
        cpar = small("cpar", 16)
        assert place[0] <= 229368, place[0]

        ident, tri = cst[:, C_IDENT:C_TRI], cst[:, C_TRI:C_HEADAVG]
        headavg, ramp = cst[:, C_HEADAVG:C_RAMP], cst[:, C_RAMP:C_MASK]
        p_n1, p_n2 = 48, 48 + KT
        p_pb = p_n2 + KT
        p_ps, p_og = p_pb + GROUPS, p_pb + 2 * GROUPS
        p_qg = p_og + NPAIR
        p_kg = p_qg + 1
        m_sc1, m_sh1, m_g1, m_sh2, m_sc2, m_g2 = (KT * v for v in range(6))

        ps = ctx.enter_context(nc.psum_tensor("ps", [P, 8, HALF], F32))

        def sem(name):
            return ctx.enter_context(nc.semaphore(name))

        s_const, s_rows, s_c, s_poolw = sem("const_in"), sem("rows_in"), sem("c_in"), sem("poolw_in")
        s_x = [sem(f"x_in{h}") for h in range(2)]
        s_ada = [sem(f"ada_in{s}") for s in range(8)]
        s_w = [sem(f"w_in{b}") for b in range(2)]
        s_wd = sem("wd_in")
        s_fill = sem("fills_done")
        s_rowsT = sem("rows_turned")
        s_pcol = sem("params_ready")
        s_cact = sem("c_act_ready")
        s_acc, s_col = sem("ada_acc_ready"), sem("ada_cols_done")
        s_mod = sem("mod_ready")
        s_xps, s_xev, s_sqx, s_ssum = sem("xT_in_psum"), sem("xT_evacuated"), sem("sqx_ready"), sem("ssum_added")
        s_ms, s_msread, s_rstd = sem("meansq_ready"), sem("meansq_read"), sem("rstd_ready")
        s_t, s_ahi, s_act = sem("normed_ready"), sem("act_hi_ready"), sem("act_ready")
        s_whi, s_wlo = sem("w_hi_ready"), sem("w_split_ready")
        s_tile, s_free = sem("tile_done"), sem("proj_consumed")
        s_sq = sem("headsq_ready")
        s_vT, s_vps, s_v = sem("vT_ready"), sem("v_turned"), sem("v_tok_ready")
        s_pads, s_pooled, s_y, s_yev = sem("pads_zero"), sem("pooled_ready"), sem("y_in_psum"), sem("y_evacuated")
        s_mixhi, s_mix = sem("mix_hi_ready"), sem("mix_ready")
        s_phi, s_pair, s_vp = sem("pair_hi_ready"), sem("pair_ready"), sem("v_pair_ready")
        s_z, s_abs, s_ln, s_l = sem("z_ready"), sem("abs_ready"), sem("softlog_ready"), sem("loss_ready")
        s_r = sem("later_ready")
        s_e, s_a, s_av = sem("exponent_ready"), sem("attn_ready"), sem("attn_used")
        s_ofree = sem("o_evacuated")
        s_osq, s_on = sem("osq_ready"), sem("o_normed")
        s_sq2 = sem("sq2_ready")
        s_cpar = sem("conv_params_ready")
        s_cg, s_conv1, s_conv, s_silu = sem("conv_base_ready"), sem("conv_first_tap"), sem("conv_ready"), sem("silu_ready")
        s_full, s_ffhi, s_ff = sem("ff_product_ready"), sem("ff_hi_ready"), sem("ff_ready")
        s_wdhi, s_wds = sem("wd_hi_ready"), sem("wd_split_ready")
        s_down, s_dev = sem("down_done"), sem("down_evacuated")
        s_tout, s_oev = sem("out_turned"), sem("out_evacuated")
        s_out = [sem(f"out_stored{b}") for b in range(2)]
        s_dve, s_actc, s_poolc = sem("dve_chain"), sem("act_chain"), sem("pool_chain")

        w_in_v = w_in[0].rearrange("(k p) e -> p k e", p=P)
        w_out_v = w_out[0].rearrange("(k p) e -> p k e", p=P)
        w_up_v = w_up[0].rearrange("(k p) e -> p k e", p=P)
        w_dn_v = w_down[0].rearrange("(k p) e -> p k e", p=P)
        ada_v = ada_w[0].rearrange("(p k) n -> p k n", k=KT)

        def banks(n):
            return ps[:, 2 * (n % 2):2 * (n % 2) + 2, :]

        def flat(ap):
            return ap.rearrange("p a b -> p (a b)")

        ms_ps = flat(ps[:, 4:6, :])
        block = ctx.enter_context(nc.Block())

        @block.sync
        def _(sp):
            def load_x(h):
                sp.dma_start(x_tok[:, 4 * h:4 * h + 4, :],
                             x[0, HALF * h:HALF * h + HALF, :].rearrange("(j p) d -> p j d", p=P)).then_inc(s_x[h], 16)

            def load_first(pc):
                lo = D + 256 * pc if pc < 4 else 256 * (pc - 4)
                sp.dma_start(ada_piece[pc][:, :, :], ada_v[:, :, lo:lo + 256]).then_inc(s_ada[pc], 16)

            sp.dma_start(cst[:, :], consts[:, 0:C_MASK]).then_inc(s_const, 16)
            sp.dma_start(c_raw[:, :], c.rearrange("b (p k) -> (b p) k", k=KT)).then_inc(s_c, 16)
            load_x(0)
            load_first(0)
            load_x(1)
            load_first(1)
            rows = [(ada_b[0], 0, 48), (norm1_g[0], p_n1, KT), (norm2_g[0], p_n2, KT),
                    (pool_b[0].rearrange("g d -> (g d)"), p_pb, GROUPS), (pool_scale[0], p_ps, GROUPS),
                    (attn_out_g[0].rearrange("h d -> (h d)"), p_og, NPAIR)]
            for src, r, n in rows:
                sp.dma_start(prow[r:r + n, 0, :], src.rearrange("(r f) -> r f", f=P)).then_inc(s_rows, 16)
            for g, r in ((q_norm_g, p_qg), (k_norm_g, p_kg)):
                for h in range(2):
                    sp.dma_start(prow[r:r + 1, 0, 64 * h:64 * h + 64], g).then_inc(s_rows, 16)
            cw = conv_w[0].rearrange("j (m f) -> (j m) f", f=P)
            cb = conv_b[0].rearrange("(m f) -> m f", f=P)
            sp.dma_start(prow[0:4 * FT, 1, :], cw[0:4 * FT, :]).then_inc(s_rows, 16)
            sp.dma_start(prow[0:2 * FT, 2, :], cw[4 * FT:6 * FT, :]).then_inc(s_rows, 16)
            sp.dma_start(prow[2 * FT:4 * FT, 2, :], cb).then_inc(s_rows, 16)
            sp.dma_start(maskf[:, :], consts[:, C_MASK:C_END]).then_inc(s_const, 16)
            for pc in range(2, 8):
                load_first(pc)
            for n in range(2):
                sp.dma_start(w_raw[n][:, :, :], w_in_v[:, :, P * n:P * n + P]).then_inc(s_w[n], 16)

            def load_piece(pc, parity):
                sp.wait_ge(s_acc, 2 * pc - 2)
                sp.dma_start(ada_piece[4 + parity][:, :, :],
                             ada_v[:, :, ds(pc * 256, 256)]).then_inc(s_ada[4 + parity], 16)

            def load_tile(n, parity, src, col):
                sp.wait_ge(s_wlo, n - 1)
                sp.dma_start(w_raw[parity][:, :, :], src[:, :, ds(col, P)]).then_inc(s_w[parity], 16)

            for n in range(2, 4):
                load_tile(n, n % 2, w_in_v, n * P)
            sp.wait_ge(s_acc, 16)
            sp.dma_start(wpool[:, :].rearrange("p (g d) -> p g d", g=GROUPS),
                         pool_w[0].rearrange("g c d -> c g d")).then_inc(s_poolw, 16)
            load_piece(8, 0)
            load_piece(9, 1)
            for n in range(4, T_Q + 4):
                load_tile(n, n % 2, w_in_v, n * P)
            with sp.Fori(0, NPAIR - 1) as j:
                for b in range(2):
                    load_tile(2 * j + (T_Q + 4 + b), b, w_in_v, (2 * j + (T_Q + 4 + b)) * P)
                    load_piece(4 * j + (10 + 2 * b), 0)
                    load_piece(4 * j + (11 + 2 * b), 1)
            load_tile(N_IN - 2, 0, w_in_v, (N_IN - 2) * P)
            load_piece(22, 0)
            load_piece(23, 1)
            load_tile(N_IN - 1, 1, w_in_v, (N_IN - 1) * P)
            with sp.Fori(0, KT // 2) as j:
                for b in range(2):
                    load_tile(2 * j + (T_OUT + b), b, w_out_v, (2 * j + b) * P)
            for b in range(2):
                load_tile(T_UP + b, b, w_up_v, b * DFF)
            sp.wait_ge(s_on, NPAIR)
            sp.dma_start(wd_raw[:, :, :], w_dn_v[:, 0:2, :]).then_inc(s_wd, 16)

            with sp.Fori(0, NG - 1) as g:
                load_tile(4 * g + (T_UP + 2), 0, w_up_v, (2 * g + 1) * P)
                load_tile(4 * g + (T_UP + 3), 1, w_up_v, (2 * g + 1) * P + DFF)
                load_tile(4 * g + (T_UP + 4), 0, w_up_v, (2 * g + 2) * P)
                load_tile(4 * g + (T_UP + 5), 1, w_up_v, (2 * g + 2) * P + DFF)
                sp.wait_ge(s_wds, g + 1)
                sp.dma_start(wd_raw[:, :, :], w_dn_v[:, ds(2 * g + 2, 2), :]).then_inc(s_wd, 16)
            load_tile(T_UP + 4 * NG - 2, 0, w_up_v, (FT - 1) * P)
            load_tile(T_UP + 4 * NG - 1, 1, w_up_v, (FT - 1) * P + DFF)
            for m in range(KT):
                sp.wait_ge(s_oev, m + 1)
                sp.dma_start(out[0].rearrange("(j p) d -> p j d", p=P)[:, :, P * m:P * m + P],
                             o_sb[m % 2][:, :, :]).then_inc(s_out[m % 2], 16)
            for b in range(2):
                sp.wait_ge(s_out[b], 16 * (KT // 2))

        @block.gpsimd
        def _(pool):
            g_ = nc.gpsimd
            chained = [0]

            g_.memset(negones[:, :], -1.0).then_inc(s_fill, 1)
            g_.memset(ones[:, :], 1.0).then_inc(s_fill, 1)
            g_.memset(one[:, :], 1.0).then_inc(s_fill, 1)

            def low_part(n, b):
                pool.wait_ge(s_whi, n + 1)
                g_.tensor_tensor(w_lo[b][:, :, :], w_raw[b][:, :, :], w_hi[b][:, :, :].bitcast(F32),
                                 ALU.subtract).then_inc(s_wlo, 1)

            for h in range(2):
                for k in range(1, KT):
                    u = h * KT + k
                    pool.wait_ge(s_sqx, u + 1)
                    if k > 1:
                        pool.wait_ge(s_ssum, h * (KT - 1) + k - 1)
                    cols = slice(HALF * h, HALF * h + HALF)
                    g_.tensor_tensor(ssum[:, cols], ssum[:, cols], sqx[u % 2][:, :], ALU.add).then_inc(s_ssum, 1)
            low_part(0, 0)
            low_part(1, 1)
            pool.wait_ge(s_act, KT)
            for t in (*u_pad, *wsum):
                g_.memset(t[:, 0:PAD], 0.0).then_inc(s_pads, 1)
            for n in range(2, N_IN + 2):
                low_part(n, n % 2)
            with pool.Fori(0, NPAIR // 2) as it:
                def pair_low(b):
                    pool.wait_ge(s_phi, 4 * it + (2 * b + 1))
                    g_.tensor_tensor(ql[b][:, :], kq_f[:, ds((2 * it + b) * S, S)], qh[b][:, :].bitcast(F32),
                                     ALU.subtract).then_inc(s_pair, 1)
                    pool.wait_ge(s_phi, 4 * it + (2 * b + 2))
                    g_.tensor_tensor(kl[b][:, :], kq_f[:, ds((2 * it + (NPAIR + b)) * S, S)], kh[b][:, :].bitcast(F32),
                                     ALU.subtract).then_inc(s_pair, 1)

                pair_low(0)
                for n in range(NB):
                    par, h, i = BODY[n]
                    if n == 2:
                        pair_low(1)
                    if i == 0:
                        continue
                    pool.wait_ge(s_l, it * NB + n + 1)
                    if n:
                        pool.wait_ge(s_e, it * NB + n)
                    new, old = col0(n), HALF
                    if i != 4 * h + 3:
                        pool.wait_ge(s_r, it * ADDS_BEFORE[NB] + ADDS_BEFORE[n])
                        old = col0(n - 1)
                        ins = g_.tensor_tensor(later[(n + 1) % 2][:, old:HALF], later[n % 2][:, old:HALF],
                                               loss[n % 3][:, old:HALF], ALU.subtract)
                    if new < old:
                        ins = g_.tensor_tensor(later[(n + 1) % 2][:, new:old], loss[n % 3][:, new:old],
                                               negones[:, 0:old - new], ALU.mult)
                    ins.then_inc(s_r, 1)

            for p in range(NPAIR):
                pool.wait_ge(s_ahi, KT + p + 1)
                g_.tensor_tensor(act_lo[:, NPAIR + p, :], on[p % 2][:, :], act_hi[:, NPAIR + p, :].bitcast(F32),
                                 ALU.subtract).then_inc(s_mix, 1)
            for m in range(KT):
                if m:
                    pool.wait_ge(s_sq2, m + 1)
                    if m > 1:
                        pool.wait_ge(s_ssum, 2 * (KT - 1) + m - 1)
                    g_.tensor_tensor(ssum[:, :], ssum[:, :], sq2[m % 2][:, :], ALU.add).then_inc(s_ssum, 1)
                low_part(T_OUT + m + 2, m % 2)

            def group(g, last):
                n = 4 * g + T_UP
                low_part(n + 2, 0)
                low_part(n + 3, 1)
                low_ff(2 * g, 0)
                if not last:
                    low_part(n + 4, 0)
                pool.wait_ge(s_wdhi, g + 1)
                g_.tensor_tensor(wd_lo[:, :, :], wd_raw[:, :, :], wd_hi[:, :, :].bitcast(F32),
                                 ALU.subtract).then_inc(s_wds, 1)
                if not last:
                    low_part(n + 5, 1)
                low_ff(2 * g + 1, 1)

            def low_ff(f, b):
                pool.wait_ge(s_ffhi, f + 1)
                g_.tensor_tensor(ff_lo[:, b, :], cval[b][:, :], ff_hi[:, b, :].bitcast(F32),
                                 ALU.subtract).then_inc(s_ff, 1)

            with pool.Fori(0, NG - 1) as g:
                group(g, False)
            group(NG - 1, True)

        @block.scalar
        def _(act):
            a_ = nc.scalar
            nsq = [0]

            def high_part(n, b, count):
                act.wait_ge(s_w[b], 16 * count)
                a_.activation(w_hi[b][:, :, :], w_raw[b][:, :, :], ACT.Identity).then_inc(s_whi, 1)

            def rstd(dst, src, r, scale=1.0):
                act.wait_ge(s_ms, r + 1)
                a_.activation(dst, src, ACT.Ln, bias=EPS, scale=scale).then_inc(s_msread, 1)
                act.wait_ge(s_msread, r + 1)
                a_.activation(dst, dst, ACT.Exp, scale=-0.5).then_inc(s_rstd, 1)

            act.wait_ge(s_c, 16)
            a_.activation(c_act[:, :], c_raw[:, :], ACT.Silu).then_inc(s_cact, 1)
            act.preload_act_table_set("natural_log_exp_and_others")
            for h in range(2):
                for k in range(KT):
                    u = h * KT + k
                    act.wait_ge(s_xps, u + 1)
                    a_.activation(xT[:, k, HALF * h:HALF * h + HALF], ps[:, u % 4, :], ACT.Identity)
                    last = max((q for q in range(u) if k and q % KT and q % 2 == u % 2), default=0)
                    if last:
                        act.wait_ge(s_ssum, last - last // KT)
                    dst = ssum[:, HALF * h:HALF * h + HALF] if k == 0 else sqx[u % 2][:, :]
                    a_.activation(dst, ps[:, u % 4, :], ACT.Square).then_inc(s_sqx, 1)
            high_part(0, 0, 1)
            high_part(1, 1, 1)
            rstd(ssum[:, :], ms_ps, 0, 1.0 / D)
            for k in range(KT):
                act.wait_ge(s_t, k + 1)
                a_.activation(act_hi[:, k, :], tnorm[k % 2][:, :], ACT.Identity,
                              bias=modc[:, m_sh1 + k:m_sh1 + k + 1]).then_inc(s_ahi, 1)
            for i in range(N_IN):
                act.wait_ge(s_tile, i + 1)
                r = i - T_Q
                if T_Q <= i < T_V:
                    if i == T_Q + 1:
                        act.wait_ge(s_pooled, GROUPS)
                    if r >= 2:
                        act.wait_ge(s_free, i - 1)
                    a_.activation(hn[r % 2][:, :], flat(banks(i)), ACT.Square).then_inc(s_sq, 1)
                high_part(i + 2, i % 2, i // 2 + 2)
                if T_Q <= i < T_V:
                    rstd(hn[r % 2][:, :], ms_ps, 1 + r)
            act.wait_ge(s_yev, GROUPS)
            for g in range(GROUPS):
                a_.activation(act_hi[:, g, :], u_pad[g][:, PAD:], ACT.Identity).then_inc(s_mixhi, 1)

            with act.Fori(0, NPAIR // 2) as it:
                def weights(n):
                    act.wait_ge(s_e, it * NB + n + 1)
                    if n >= 3:
                        act.wait_ge(s_av, it * NB + n - 2)
                    cols = slice(col0(n), HALF)
                    a_.activation(attn[n % 3][:, cols], ps[:, n % 6, cols], ACT.Exp).then_inc(s_a, 1)

                for n in range(NB):
                    cols = slice(col0(n), HALF)
                    act.wait_ge(s_abs, it * NB + n + 1)
                    a_.activation(soft[n % 3][:, cols], soft[n % 3][:, cols], ACT.Exp, scale=-1.0).then_inc(s_actc, 1)
                    act.wait_ge(s_actc, it * NB + n + 1)
                    a_.activation(soft[n % 3][:, cols], soft[n % 3][:, cols], ACT.Ln, bias=1.0).then_inc(s_ln, 1)
                    if n >= 3:
                        weights(n - 3)
                for n in range(NB - 3, NB):
                    weights(n)

            act.wait_ge(s_ofree, 4 * NPAIR)
            for p in range(NPAIR):
                a_.activation(osq[p][:, :], kq[:, NPAIR + p, :], ACT.Square).then_inc(s_osq, 1)
            for p in range(NPAIR + 1):
                if p < NPAIR:
                    rstd(osq[p][:, :], flat(ps[:, 4 + 2 * (p % 2):6 + 2 * (p % 2), :]), 1 + 2 * NPAIR + p)
                if p:
                    act.wait_ge(s_on, p)
                    a_.activation(act_hi[:, NPAIR + p - 1, :], on[(p - 1) % 2][:, :], ACT.Identity).then_inc(s_ahi, 1)
            for m in range(KT):
                n = T_OUT + m
                act.wait_ge(s_free, n + 1)
                if m >= 3:
                    act.wait_ge(s_ssum, 2 * (KT - 1) + m - 2)
                a_.activation(ssum[:, :] if m == 0 else sq2[m % 2][:, :], xT[:, m, :], ACT.Square).then_inc(s_sq2, 1)
                high_part(n + 2, n % 2, n // 2 + 2)
            rstd(ssum[:, :], ms_ps, 1 + 3 * NPAIR, 1.0 / D)
            for k in range(KT):
                act.wait_ge(s_t, KT + k + 1)
                a_.activation(act_hi[:, k, :], t2[k % 2][:, :], ACT.Identity,
                              bias=modc[:, m_sh2 + k:m_sh2 + k + 1]).then_inc(s_ahi, 1)

            act.preload_act_table_set("silu_and_others")

            def group(g, last, first):
                n0 = 4 * g + T_UP
                act.wait_ge(s_cpar, g + 1)
                for b in range(2):
                    f = 2 * g + b
                    for half, dst in ((0, cgate), (1, cval)):
                        n = n0 + (2 * b + half)
                        act.wait_ge(s_tile, n + 1)
                        if half and not first:
                            act.wait_ge(s_ff, f - 1)
                        v = cpar[:, :].rearrange("p (j h b) -> p j h b", j=4, h=2)
                        a_.activation(dst[b][:, :], flat(banks(half)), ACT.Identity,
                                      scale=v[:, 2, half, b:b + 1], bias=v[:, 3, half, b:b + 1]).then_inc(s_cg, 1)
                        if not (last and b == 1):
                            high_part(n + 2, half, 2 * g + ((T_UP + 2 * b) // 2 + 2))
                    act.wait_ge(s_conv, 2 * f + 1)
                    if not first:
                        act.wait_ge(s_full, f - 1)
                    a_.activation(silu[b][:, :], cgate[b][:, :], ACT.Silu).then_inc(s_silu, 1)
                    if b == 1:
                        act.wait_ge(s_wd, 16 * g + 16)
                        a_.activation(wd_hi[:, :, :], wd_raw[:, :, :], ACT.Identity).then_inc(s_wdhi, 1)
                    act.wait_ge(s_full, f + 1)
                    if not first and b == 0:
                        act.wait_ge(s_down, 8 * g)
                    a_.activation(ff_hi[:, b, :], cval[b][:, :], ACT.Identity).then_inc(s_ffhi, 1)

            group(0, False, True)
            with act.Fori(1, NG - 1) as g:
                group(g, False, False)
            group(NG - 1, True, False)
            for m in range(KT):
                act.wait_ge(s_tout, m + 1)
                if m >= 2:
                    act.wait_ge(s_out[m % 2], 16 * (m // 2))
                a_.activation(o_sb[m % 2][:, :, :].rearrange("p j d -> p (j d)"), flat(banks(m)),
                              ACT.Identity).then_inc(s_oev, 1)

        @block.vector
        def _(dve):
            v_ = nc.vector
            done = [0]

            def link(ins):
                done[0] += 1
                ins.then_inc(s_dve, 1)
                dve.wait_ge(s_dve, done[0])

            def parameters():
                dve.wait_ge(s_const, 32)
                v_.tensor_copy(ident_b[:, :], ident).then_inc(s_pcol, 1)
                v_.tensor_copy(mask_b[:, :], maskf[:, :]).then_inc(s_pcol, 1)
                dve.wait_ge(s_rowsT, 1)
                link(v_.tensor_copy(pcol[:, :], ps[:, 7, 0:NPAR + 8 * FT]))
                v_.tensor_scalar(qg8[:, :], pcol[:, p_qg:p_qg + 1], 0.125, None, ALU.mult).then_inc(s_pcol, 1)

            dve.wait_ge(s_cact, 1)

            def piece(pc, slot, count):
                dve.wait_ge(s_ada[slot], 16 * count)
                dst = acc_first[pc % 2] if pc < 8 else acc
                free = pc - 1 if pc < 8 else pc
                if free > 0:
                    dve.wait_ge(s_col, free)
                    dve.wait_ge(s_acc, 2 * free)
                src = ada_piece[slot]
                for k in range(KT):
                    half = dst[:, 256 * (k % 2):256 * (k % 2) + 256]
                    if k < 2:
                        ins = v_.tensor_scalar(half, src[:, k, :], c_act[:, k:k + 1], None, ALU.mult)
                    else:
                        dve.wait_ge(s_dve, done[0] - (k < KT - 1))
                        ins = v_.scalar_tensor_tensor(out=half, in0=src[:, k, :], scalar=c_act[:, k:k + 1],
                                                      in1=half, op0=ALU.mult, op1=ALU.add)
                    if k < KT - 2:
                        ins.then_inc(s_dve, 1)
                        done[0] += 1
                    else:
                        ins.then_inc(s_acc, 1)

            for pc in range(8):
                piece(pc, pc, 1)
                if pc == 5:
                    parameters()
            dve.wait_ge(s_col, 8)
            link(v_.tensor_tensor(modc[:, m_sc1:m_sc1 + KT], ps[:, 6, 0:KT], pcol[:, KT:2 * KT], ALU.add))
            v_.tensor_tensor(modc[:, m_sh1:m_sh1 + KT], ps[:, 6, KT:2 * KT], pcol[:, 0:KT], ALU.add).then_inc(s_mod, 1)
            link(v_.scalar_tensor_tensor(out=gain[:, 0:KT], in0=modc[:, m_sc1:m_sc1 + KT], scalar=1.0,
                                         in1=pcol[:, p_n1:p_n1 + KT], op0=ALU.add, op1=ALU.mult))
            dve.wait_ge(s_mod, 1)

            def norm(tmp, gcol, shift, r, base, before):
                dve.wait_ge(s_rstd, r + 1)
                for k in range(KT + 1):
                    if k >= 2:
                        dve.wait_ge(s_act, before + k - 1)
                    if k < KT:
                        v_.scalar_tensor_tensor(out=tmp[k % 2][:, :], in0=xT[:, k, :], scalar=gain[:, gcol + k:gcol + k + 1],
                                                in1=ssum[:, :], op0=ALU.mult, op1=ALU.mult).then_inc(s_t, 1)
                    if k:
                        q = k - 1
                        dve.wait_ge(s_ahi, base + q + 1)
                        v_.scalar_tensor_tensor(out=act_lo[:, q, :], in0=tmp[q % 2][:, :],
                                                scalar=modc[:, shift + q:shift + q + 1],
                                                in1=act_hi[:, q, :].bitcast(F32), op0=ALU.add,
                                                op1=ALU.subtract).then_inc(s_act, 1)

            norm(tnorm, 0, m_sh1, 0, 0, 0)

            def pooled_output(g):
                dve.wait_ge(s_y, g + 1)
                v_.tensor_scalar(u_pad[g][:, PAD:], flat(ps[:, 6:8, :]), pcol[:, p_pb + g:p_pb + g + 1],
                                 pcol[:, p_ps + g:p_ps + g + 1], ALU.add, ALU.mult).then_inc(s_yev, 1)

            for i in range(N_IN):
                r = i - T_Q
                if 0 <= r < 2 * NPAIR:
                    piece(8 + 2 * r, 4, r + 2)
                dve.wait_ge(s_tile, i + 1)
                if i < T_Q:
                    g, w = i, POOL_WINDOWS[i]
                    if i == 0:
                        dve.wait_ge(s_pads, 6)
                    v_.tensor_copy(u_pad[g][:, PAD:], flat(banks(i))).then_inc(s_free, 1)
                    dve.wait_ge(s_free, i + 1)
                    cur, step, b = u_pad[g], 1, 0
                    while step < w:
                        link(v_.tensor_tensor(wsum[b][:, PAD:], cur[:, PAD:], cur[:, PAD - step:PAD + S - step], ALU.add))
                        cur, step, b = wsum[b], 2 * step, 1 - b
                    link(v_.scalar_tensor_tensor(out=cur[:, PAD:PAD + w], in0=cur[:, PAD:PAD + w], scalar=w / PAD,
                                                 in1=ramp[:, 0:w], op0=ALU.mult, op1=ALU.mult))
                    v_.scalar_tensor_tensor(out=u_pad[g][:, PAD:], in0=cur[:, PAD:], scalar=1.0 / w,
                                            in1=u_pad[g][:, PAD:], op0=ALU.mult, op1=ALU.subtract).then_inc(s_pooled, 1)
                    if i:
                        pooled_output(i - 1)
                    if i == T_Q - 1:
                        pooled_output(i)
                elif i < T_V:
                    dve.wait_ge(s_rstd, r + 2)
                    g = qg8[:, :] if i < T_K else pcol[:, p_kg:p_kg + 1]
                    v_.scalar_tensor_tensor(out=kq[:, r, :], in0=flat(banks(i)), scalar=g, in1=hn[r % 2][:, :],
                                            op0=ALU.mult, op1=ALU.mult).then_inc(s_free, 1)
                    piece(9 + 2 * r, 5, r + 2)
                    if i == T_V - 1:
                        dve.wait_ge(s_col, 24)
                        v_.tensor_tensor(modc[:, 2 * KT:6 * KT], ps[:, 6, 2 * KT:6 * KT], pcol[:, 2 * KT:6 * KT],
                                         ALU.add).then_inc(s_mod, 1)
                        dve.wait_ge(s_mod, 2)
                        link(v_.scalar_tensor_tensor(out=gain[:, KT:2 * KT], in0=modc[:, m_sc2:m_sc2 + KT], scalar=1.0,
                                                     in1=pcol[:, p_n2:p_n2 + KT], op0=ALU.add, op1=ALU.mult))
                else:
                    q = i - T_V
                    if q >= 2:
                        dve.wait_ge(s_vps, q - 1)
                    v_.tensor_copy(hn[q % 2][:, :], flat(banks(i))).then_inc(s_free, 1)
                    dve.wait_ge(s_vps, q + 1)
                    v_.tensor_copy(v_tok[:, :, P * q:P * q + P], ms_ps.rearrange("p (j d) -> p j d", j=SB)).then_inc(s_v, 1)
            dve.wait_ge(s_v, NPAIR)
            dve.wait_ge(s_free, N_IN)
            for g in range(GROUPS):
                dve.wait_ge(s_mixhi, g + 1)
                v_.tensor_tensor(act_lo[:, g, :], u_pad[g][:, PAD:], act_hi[:, g, :].bitcast(F32),
                                 ALU.subtract).then_inc(s_mix, 1)

            with dve.Fori(0, NPAIR // 2) as it:
                def pair_high(b):
                    v_.tensor_scalar(qh[b][:, :], kq_f[:, ds((2 * it + b) * S, S)], 1.0, None, ALU.mult).then_inc(s_phi, 1)
                    v_.tensor_scalar(kh[b][:, :], kq_f[:, ds((2 * it + (NPAIR + b)) * S, S)], 1.0, None,
                                     ALU.mult).then_inc(s_phi, 1)
                    v_.tensor_scalar(vp[b][:, :, :], v_tok[:, :, ds(it * 2 * P + b * P, P)], 1.0, None,
                                     ALU.mult).then_inc(s_vp, 1)

                def losses(n):
                    cols = slice(col0(n), HALF)
                    dve.wait_ge(s_ln, it * NB + n + 1)
                    if n >= 3:
                        dve.wait_ge(s_e, it * NB + n - 2)
                        if ADDS_BEFORE[n - 2]:
                            dve.wait_ge(s_r, it * ADDS_BEFORE[NB] + ADDS_BEFORE[n - 2])
                    v_.scalar_tensor_tensor(out=loss[n % 3][:, cols], in0=ps[:, n % 6, cols], scalar=0.0,
                                            in1=soft[n % 3][:, cols], op0=ALU.max, op1=ALU.add).then_inc(s_l, 1)

                def evacuate(s):
                    par, h, _ = BODY[LAST_OF[s]]
                    pair = s // (NSEQ // 2)
                    rows = slice(64 * par, 64 * par + 64)
                    dve.wait_ge(s_av, it * NB + LAST_OF[s] + 1)
                    v_.tensor_scalar(kq_f[rows, ds((2 * it + (NPAIR + pair)) * S + HALF * h, HALF)],
                                     ps[rows, 6 + s % 2, :], 1.0, None, ALU.mult).then_inc(s_ofree, 1)

                pair_high(0)
                for n in range(NB):
                    cols = slice(col0(n), HALF)
                    dve.wait_ge(s_z, it * NB + n + 1)
                    if n >= 3:
                        dve.wait_ge(s_l, it * NB + n - 2)
                    v_.tensor_scalar(soft[n % 3][:, cols].bitcast(U32), ps[:, n % 6, cols].bitcast(U32), ABS_BITS, None,
                                     ALU.bitwise_and).then_inc(s_abs, 1)
                    if n:
                        losses(n - 1)
                    if n == 2:
                        dve.wait_ge(s_mix, GROUPS)
                        pair_high(1)
                    for s in range(NSEQ):
                        if LAST_OF[s] + 5 == n:
                            evacuate(s)
                losses(NB - 1)
                evacuate(NSEQ - 1)

            for p in range(NPAIR):
                dve.wait_ge(s_rstd, 2 + 2 * NPAIR + p)
                if p >= 2:
                    dve.wait_ge(s_mix, GROUPS + p - 1)
                v_.scalar_tensor_tensor(out=on[p % 2][:, :], in0=kq[:, NPAIR + p, :], scalar=pcol[:, p_og + p:p_og + p + 1],
                                        in1=osq[p][:, :], op0=ALU.mult, op1=ALU.mult).then_inc(s_on, 1)
            for m in range(KT):
                dve.wait_ge(s_tile, T_OUT + m + 1)
                v_.scalar_tensor_tensor(out=xT[:, m, :], in0=flat(banks(m)), scalar=modc[:, m_g1 + m:m_g1 + m + 1],
                                        in1=xT[:, m, :], op0=ALU.mult, op1=ALU.add).then_inc(s_free, 1)
            dve.wait_ge(s_free, T_OUT + KT)
            norm(t2, KT, m_sh2, 1 + 3 * NPAIR, KT + NPAIR, KT)

            conv_v = pcol[:, NPAR:NPAR + 8 * FT].rearrange("p (j h f) -> p j h f", j=4, h=2)

            def group(g, first):
                if not first:
                    dve.wait_ge(s_cg, 4 * g)
                if not (isinstance(g, int) and g < 2):
                    dve.wait_ge(s_dev, 8 * g - 8)
                v_.tensor_scalar(cpar[:, :].rearrange("p (j h b) -> p j h b", j=4, h=2),
                                 conv_v[:, :, :, ds(2 * g, 2)], 1.0, None, ALU.mult).then_inc(s_cpar, 1)
                dve.wait_ge(s_cpar, g + 1)
                for b in range(2):
                    for half, dst in ((0, cgate), (1, cval)):
                        v = cpar[:, :].rearrange("p (j h b) -> p j h b", j=4, h=2)
                        r = 2 * b + half
                        src = flat(banks(half))
                        dve.wait_ge(s_cg, 4 * g + (r + 1))
                        v_.scalar_tensor_tensor(out=dst[b][:, 1:S], in0=src[:, 0:S - 1], scalar=v[:, 1, half, b:b + 1],
                                                in1=dst[b][:, 1:S], op0=ALU.mult, op1=ALU.add).then_inc(s_conv1, 1)
                        dve.wait_ge(s_conv1, 4 * g + (r + 1))
                        v_.scalar_tensor_tensor(out=dst[b][:, 2:S], in0=src[:, 0:S - 2], scalar=v[:, 0, half, b:b + 1],
                                                in1=dst[b][:, 2:S], op0=ALU.mult, op1=ALU.add).then_inc(s_conv, 1)
                    dve.wait_ge(s_conv, 4 * g + (2 * b + 2))
                    dve.wait_ge(s_silu, 2 * g + (b + 1))
                    v_.tensor_tensor(cval[b][:, :], cval[b][:, :], silu[b][:, :], ALU.mult).then_inc(s_full, 1)
                    if b == 0 and not first:
                        for m in range(KT):
                            evac_down(8 * g - 8, m)

            def evac_down(base, m):
                dve.wait_ge(s_down, base + (m + 1))
                v_.scalar_tensor_tensor(out=xT[:, m, :], in0=flat(ps[:, 4 + 2 * (m % 2):6 + 2 * (m % 2), :]),
                                        scalar=modc[:, m_g2 + m:m_g2 + m + 1], in1=xT[:, m, :], op0=ALU.mult,
                                        op1=ALU.add).then_inc(s_dev, 1)

            group(0, True)
            group(1, False)
            with dve.Fori(2, NG) as g:
                group(g, False)
            dve.wait_ge(s_dev, 8 * NG - 8)
            for m in range(KT):
                evac_down(8 * NG - 8, m)

        @block.tensor
        def _(pe):
            t_ = nc.tensor

            def product(n, b, ks, moving_ready=None):
                for k in ks:
                    if moving_ready is not None:
                        pe.wait_ge(*moving_ready(k))
                    o0, o1 = (ps[:, 2 * b + h, :] for h in range(2))
                    seq = [(w_hi, act_hi, 0), (w_hi, act_hi, 1), (w_hi, act_lo, 0), (w_hi, act_lo, 1),
                           (w_lo, act_hi, 0), (w_lo, act_hi, 1)]
                    for j, (w, a, h) in enumerate(seq):
                        mm = t_.matmul(ps[:, 2 * b + h, :], w[b][:, k, :], a[:, k, HALF * h:HALF * h + HALF],
                                       start=(k == 0 and j < 2), stop=(k == KT - 1 and j >= 4))
                return mm

            def begin(n):
                pe.wait_ge(s_wlo, n + 1)
                if not isinstance(n, int) or n >= 2:
                    pe.wait_ge(s_free, n - 1)

            def begin_up(n):
                pe.wait_ge(s_wlo, n + 1)
                pe.wait_ge(s_conv, n - (T_UP + 1))

            def tile(n, b, begin=begin):
                begin(n)
                product(n, b, range(KT)).then_inc(s_tile, 1)

            def ada_cols(pc, col, acc=acc):
                pe.wait_ge(s_acc, 2 * pc + 2)
                for h in range(2):
                    dst = ps[:, 6, col + h:col + h + 1] if isinstance(col, int) else ps[:, 6, ds(col + h, 1)]
                    for e in range(2):
                        mm = t_.matmul(dst, acc[:, 256 * e + P * h:256 * e + P * h + P], one[:, :],
                                       start=(e == 0), stop=(e == 1))
                mm.then_inc(s_col, 1)

            def means(weights, src, bank):
                for h in range(2):
                    mm = t_.matmul(ps[:, bank + h, :], weights, src[:, HALF * h:HALF * h + HALF], start=True, stop=True)
                mm.then_inc(s_ms, 1)

            def turn_x(h):
                pe.wait_ge(s_x[h], 16)
                for k in range(KT):
                    u = h * KT + k
                    if u >= 4:
                        pe.wait_ge(s_sqx, u - 3)
                    for j in range(4):
                        mm = t_.transpose(ps[:, u % 4, P * j:P * j + P], x_tok[:, 4 * h + j, P * k:P * k + P], ident)
                    mm.then_inc(s_xps, 1)

            pe.wait_ge(s_const, 16)
            turn_x(0)
            turn_x(1)
            pe.wait_ge(s_rows, 16 * 13)
            for j, (r, lo) in enumerate(((NPAR, 0), (4 * FT, NPAR), (4 * FT, NPAR + 4 * FT))):
                mm = t_.transpose(ps[:, 7, lo:lo + r], prow[0:r, j, :], ident[0:r, 0:r])
            mm.then_inc(s_rowsT, 1)
            pe.wait_ge(s_fill, 3)
            for pc in range(4):
                ada_cols(pc, 2 * pc, acc_first[pc % 2])
            pe.wait_ge(s_ssum, 2 * (KT - 1))
            means(ones[:, :], ssum, 4)
            for pc in range(4, 8):
                ada_cols(pc, 2 * pc, acc_first[pc % 2])

            begin(0)
            begin(1)
            for k in range(KT):
                m0 = product(0, 0, [k], lambda k: (s_act, k + 1))
                m1 = product(1, 1, [k])
                if k == KT - 1:
                    m0.then_inc(s_tile, 1)
                    m1.then_inc(s_tile, 1)

            def group_map(g):
                pe.wait_ge(s_pooled, g + 1)
                if g:
                    pe.wait_ge(s_yev, g)
                for h in range(2):
                    mm = t_.matmul(ps[:, 6 + h, :], wpool[:, P * g:P * g + P],
                                   u_pad[g][:, PAD + HALF * h:PAD + HALF * h + HALF], start=True, stop=True)
                mm.then_inc(s_y, 1)

            pe.wait_ge(s_mod, 1)
            pe.wait_ge(s_poolw, 16)
            for n in range(2, T_Q + 1):
                begin(n)
                product(n, n % 2, range(0, 4))
                group_map(n - 2)
                product(n, n % 2, range(4, KT)).then_inc(s_tile, 1)
            group_map(GROUPS - 1)
            pe.wait_ge(s_yev, GROUPS)

            def with_means(r, n, b, col, first=False):
                begin(n)
                product(None, b, range(0, 2))
                pe.wait_ge(s_sq, r + 1)
                pe.wait_ge(s_msread, r + 1)
                means(headavg, hn[1 - b], 4)
                product(None, b, range(2, 5))
                ada_cols(2 * r + 8, col)
                product(None, b, range(5, KT)).then_inc(s_tile, 1)
                ada_cols(2 * r + 9, col + 2)

            with pe.Fori(0, NPAIR) as j:
                with_means(2 * j, 2 * j + (T_Q + 1), 1, 8 * j + 16)
                with_means(2 * j + 1, 2 * j + (T_Q + 2), 0, 8 * j + 20)
            pe.wait_ge(s_msread, 1 + 2 * NPAIR)

            def turn_v(q):
                pe.wait_ge(s_free, T_V + q + 1)
                if q:
                    pe.wait_ge(s_v, q)
                for j in range(SB):
                    mm = t_.transpose(ps[:, 4 + j // 4, P * (j % 4):P * (j % 4) + P], hn[q % 2][:, P * j:P * j + P], ident)
                mm.then_inc(s_vps, 1)

            for q in range(1, NPAIR + 1):
                if q < NPAIR:
                    begin(T_V + q)
                    product(None, q % 2, range(0, 3))
                turn_v(q - 1)
                if q < NPAIR:
                    product(None, q % 2, range(3, KT)).then_inc(s_tile, 1)
            pe.wait_ge(s_pcol, 3)

            with pe.Fori(0, NPAIR // 2) as it:
                def scores(n):
                    par, h, i = BODY[n]
                    b = n // NU
                    if n % NU == 0:
                        pe.wait_ge(s_pair, 4 * it + (2 * b + 2))
                    if n >= 6:
                        pe.wait_ge(s_a, it * NB + n - 5)
                    rows = slice(64 * par, 64 * par + 64)
                    cols = slice(col0(n), HALF)
                    qcols = slice(HALF * h + col0(n), HALF * h + HALF)
                    keys = slice(P * i, P * i + P)
                    z = ps[:, n % 6, cols]
                    diagonal = P * i >= HALF * h
                    t_.matmul(z, kh[b][rows, keys], qh[b][rows, qcols], start=True, stop=False)
                    t_.matmul(z, kh[b][rows, keys], ql[b][rows, qcols], start=False, stop=False)
                    mm = t_.matmul(z, kl[b][rows, keys], qh[b][rows, qcols], start=False, stop=True)
                    if diagonal:
                        mm = t_.matmul(ps[:, n % 6, col0(n):col0(n) + P], ident_b[:, :], mask_b[:, :],
                                       start=False, stop=True, skip_group_check=True)
                    mm.then_inc(s_z, 1)

                def exponents(n):
                    par, h, i = BODY[n]
                    cols = slice(col0(n), HALF)
                    pe.wait_ge(s_l, it * NB + n + 1)
                    mm = t_.matmul(ps[:, n % 6, cols], tri, loss[n % 3][:, cols], start=False, stop=True,
                                   skip_group_check=True)
                    if i != 4 * h + 3:
                        pe.wait_ge(s_r, it * ADDS_BEFORE[NB] + ADDS_BEFORE[n])
                        cols = slice(col0(n - 1), HALF)
                        mm = t_.matmul(ps[:, n % 6, cols], ones[:, :], later[n % 2][:, cols], start=False, stop=True,
                                       skip_group_check=True)
                    mm.then_inc(s_e, 1)

                def outputs(n):
                    par, h, i = BODY[n]
                    b, s = n // NU, SEQ_OF[n]
                    cols = slice(col0(n), HALF)
                    if n % NU == 0:
                        pe.wait_ge(s_vp, 2 * it + (b + 1))
                    if i == 4 * h + 3 and s >= 2:
                        pe.wait_ge(s_ofree, it * NSEQ + s - 1)
                    pe.wait_ge(s_a, it * NB + n + 1)
                    mm = t_.matmul(ps[64 * par:64 * par + 64, 6 + s % 2, cols], vp[b][:, i, 64 * par:64 * par + 64],
                                   attn[n % 3][:, cols], start=(i == 4 * h + 3), stop=(i == 0), skip_group_check=True)
                    mm.then_inc(s_av, 1)

                for n in range(NB + 4):
                    if n < NB:
                        scores(n)
                    if 3 <= n < NB + 3:
                        exponents(n - 3)
                    if n >= 4:
                        outputs(n - 4)

            begin(T_OUT)
            begin(T_OUT + 1)
            def out_means(p):
                pe.wait_ge(s_osq, p + 1)
                if p >= 2:
                    pe.wait_ge(s_msread, 2 * NPAIR + p)
                means(headavg, osq[p], 4 + 2 * (p % 2))

            out_means(0)
            out_means(1)
            for k in range(KT):
                m0 = product(0, 0, [k], lambda k: (s_mix, k + 1))
                m1 = product(1, 1, [k])
                if k < 2:
                    out_means(2 + k)
            m0.then_inc(s_tile, 1)
            m1.then_inc(s_tile, 1)
            with pe.Fori(1, KT // 2) as j:
                tile(2 * j + T_OUT, 0)
                tile(2 * j + (T_OUT + 1), 1)
            pe.wait_ge(s_ssum, 3 * (KT - 1))
            pe.wait_ge(s_msread, 1 + 3 * NPAIR)
            means(ones[:, :], ssum, 4)

            def down(g, m, after=None):
                if m == 0:
                    pe.wait_ge(s_wds, g + 1)
                if not (isinstance(g, int) and 8 * g + m < 2):
                    pe.wait_ge(s_dev, 8 * g + (m - 1))
                for k in range(2):
                    if m == 0:
                        pe.wait_ge(s_ff, 2 * g + (k + 1))
                    seq = [(wd_hi, ff_hi, 0), (wd_hi, ff_hi, 1), (wd_hi, ff_lo, 0), (wd_hi, ff_lo, 1),
                           (wd_lo, ff_hi, 0), (wd_lo, ff_hi, 1)]
                    for j, (w, a, h) in enumerate(seq):
                        mm = t_.matmul(ps[:, 4 + 2 * (m % 2) + h, :], w[:, k, P * m:P * m + P],
                                       a[:, k, HALF * h:HALF * h + HALF], start=(k == 0 and j < 2),
                                       stop=(k == 1 and j >= 4))
                mm.then_inc(s_down, 1)

            begin(T_UP)
            begin(T_UP + 1)
            for k in range(KT):
                m0 = product(0, 0, [k], lambda k: (s_act, KT + k + 1))
                m1 = product(1, 1, [k])
            m0.then_inc(s_tile, 1)
            m1.then_inc(s_tile, 1)
            tile(T_UP + 2, 0, begin_up)
            tile(T_UP + 3, 1, begin_up)
            def up_and_down(g, first):
                tile(4 * g + T_UP, 0, begin_up)
                tile(4 * g + (T_UP + 1), 1, begin_up)
                for m in range(KT):
                    down(g - 1, m)
                tile(4 * g + (T_UP + 2), 0, begin_up)
                tile(4 * g + (T_UP + 3), 1, begin_up)

            up_and_down(1, True)
            with pe.Fori(2, NG) as g:
                up_and_down(g, False)
            for m in range(KT + 1):
                if m < KT:
                    down(NG - 1, m)
                if m:
                    q = m - 1
                    pe.wait_ge(s_dev, 8 * (NG - 1) + q + 1)
                    if q >= 2:
                        pe.wait_ge(s_oev, q - 1)
                    for j in range(SB):
                        mm = t_.transpose(ps[:, 2 * (q % 2) + j // 4, P * (j % 4):P * (j % 4) + P],
                                          xT[:, q, P * j:P * j + P], ident)
                    mm.then_inc(s_tout, 1)


_OUTS = [((1, 1024, 1024), 'float32')]
_INS = ['x', 'c', 'ada_w', 'ada_b', 'norm1_g', 'w_in', 'pool_w', 'pool_b', 'pool_scale', 'q_norm_g', 'k_norm_g',
        'attn_out_g', 'w_out', 'norm2_g', 'w_up', 'conv_w', 'conv_b', 'w_down']


def kernel(**inputs):
    import numpy as _np
    import concourse.bacc as _bacc
    from concourse import mybir as _mybir
    from concourse.bass_utils import run_bass_kernel_spmd as _run

    nc = _bacc.Bacc("TRN2", target_bir_lowering=False, num_devices=1)
    arrays, args = {}, []
    for name in _INS:
        a = _np.ascontiguousarray(inputs[name])
        arrays[f"in_{name}_dram"] = a
        args.append(nc.dram_tensor(f"in_{name}_dram", a.shape, _mybir.dt.from_np(a.dtype), kind="ExternalInput").ap())
    arrays["in_consts_dram"] = shape_constants()
    args.append(nc.dram_tensor("in_consts_dram", (P, C_END), F32, kind="ExternalInput").ap())
    for i, (shape, dtype) in enumerate(_OUTS):
        dt = _mybir.dt.from_np(_np.dtype(dtype))
        args.append(nc.dram_tensor(f"out_{i}_dram", shape, dt, kind="ExternalOutput").ap())
    hybrid_layer(nc, *args)
    r = _run(nc, [arrays], core_ids=[0])
    return r.results[0]["out_0_dram"]
```

```python
from contextlib import ExitStack

import concourse.bass as bass
from concourse import mybir

F32 = mybir.dt.float32
F32R = mybir.dt.float32r
BF16 = mybir.dt.bfloat16
U32 = mybir.dt.uint32
ALU = mybir.AluOpType
ACT = mybir.ActivationFunctionType
ds = bass.ds

P = 128
HALF = 512
EPS = 1e-6
POOL_WINDOWS = (2, 4, 8, 16)
PAD = max(POOL_WINDOWS)
MASKED = -1e30
ABS_BITS = 0x7FFFFFFF

C_IDENT, C_TRI, C_HEADAVG, C_RAMP, C_MASK, C_END = 0, 128, 256, 384, 400, 528


def shape_constants():
    import numpy as np
    c = np.zeros((P, C_END), np.float32)
    r = np.arange(P)
    c[:, C_IDENT:C_TRI] = np.eye(P)
    c[:, C_TRI:C_HEADAVG] = np.where(r[:, None] >= r[None, :], -1.0, 0.0)
    c[:, C_HEADAVG:C_RAMP] = (r[:, None] // 64 == r[None, :] // 64) / 64.0
    c[:, C_RAMP:C_MASK] = PAD / (np.arange(PAD) + 1.0)
    c[:, C_MASK:C_END] = np.where(r[:, None] >= r[None, :], MASKED, 0.0)
    return c


def hybrid_layer(nc, x, c, ada_w, ada_b, norm1_g, w_in, pool_w, pool_b, pool_scale, q_norm_g,
                 k_norm_g, attn_out_g, w_out, norm2_g, w_up, conv_w, conv_b, w_down, consts, out):
    S, D = x.shape[1], x.shape[2]
    KT = D // P
    DP = pool_w.shape[1] * pool_w.shape[2]
    GROUPS = pool_w.shape[1]
    D_IN = w_in.shape[2]
    DFF = w_down.shape[1]
    FT = DFF // P
    NG = FT // 2
    NPAIR = (D - DP) // P
    N_IN = D_IN // P
    T_OUT, T_UP = N_IN, N_IN + KT
    T_Q, T_K, T_V = DP // P, DP // P + NPAIR, DP // P + 2 * NPAIR
    SB = S // P
    assert S == 2 * HALF and KT == 8 and NPAIR == 4 and GROUPS == 4 and FT % 2 == 0

    UNITS = [(par, h, i) for par in range(2) for h in range(2) for i in range(4 * h + 3, -1, -1)]
    NU = len(UNITS)
    BODY = UNITS + UNITS
    NB = len(BODY)
    SEQ_OF = [sum(1 for u in BODY[:n + 1] if u[2] == 4 * u[1] + 3) - 1 for n in range(NB)]
    ADDS_BEFORE = [sum(1 for u in BODY[:n] if u[2] > 0) for n in range(NB + 1)]
    NSEQ = SEQ_OF[-1] + 1
    LAST_OF = [max(n for n in range(NB) if SEQ_OF[n] == s) for s in range(NSEQ)]
    SECOND = 6
    NEXT = NU + 6

    def col0(n):
        par, h, i = BODY[n]
        return max(0, P * i - HALF * h)

    with ExitStack() as ctx:
        KB = 1024
        X0 = (nc.sbuf_base + 31) // 32 * 32
        R1 = X0 + 32 * KB
        KQ0 = R1 + 64 * KB
        V0 = KQ0 + 32 * KB
        PB0 = V0 + 16 * KB
        W0 = PB0 + 32 * KB + 256
        C0 = W0 + 24 * KB
        place = [C0]

        def at(name, shape, dt, off):
            return nc.alloc_sbuf_tensor_at(name, shape, dt, offset=off)

        def small(name, cols, dt=F32):
            t = at(name, [P, cols], dt, place[0])
            place[0] += (cols * mybir.dt.size(dt) + 31) // 32 * 32
            return t

        xT = at("xT", [P, KT, S], F32, X0)
        act_hi = at("act_hi", [P, KT, S], F32R, R1)
        act_lo = at("act_lo", [P, KT, S], F32R, R1 + 32 * KB)
        acc_first = [at(f"acc_first{b}", [P, 512], F32, R1 + 8 * KB + 2 * KB * b) for b in range(2)]
        x_tok = at("x_tok", [P, SB, D], F32, R1 + 32 * KB)
        prow = at("param_rows", [P, 3, P], F32, R1)
        kq = at("kq", [P, 2 * NPAIR, S], F32, KQ0)
        kq_f = kq[:, :, :].rearrange("p a b -> p (a b)")
        v_tok = at("v_tok", [P, SB, NPAIR * P], F32, V0)
        ada_at = [KQ0, KQ0 + 8 * KB, KQ0 + 16 * KB, KQ0 + 24 * KB, V0, V0 + 8 * KB, PB0, PB0 + 8 * KB]
        ada_piece = [at(f"ada_piece{s}", [P, KT, 256], F32, o) for s, o in enumerate(ada_at)]
        w_raw = [at(f"w_raw{b}", [P, KT, P], F32, W0 + 4 * KB * b) for b in range(2)]
        w_hi = [at(f"w_hi{b}", [P, KT, P], F32R, W0 + 8 * KB + 4 * KB * b) for b in range(2)]
        w_lo = [at(f"w_lo{b}", [P, KT, P], F32R, W0 + 16 * KB + 4 * KB * b) for b in range(2)]
        ssum = at("ssum", [P, S], F32, PB0 + 16 * KB)
        sqx = [at(f"sqx{b}", [P, HALF], F32, PB0 + 20 * KB + 2 * KB * b) for b in range(2)]
        tnorm = [at(f"tnorm{b}", [P, S], F32, PB0 + 24 * KB + 4 * KB * b) for b in range(2)]
        UP = 4 * (PAD + S)
        u_pad = [at(f"u_pad{g}", [P, PAD + S], F32, W0 - UP * (GROUPS - g)) for g in range(GROUPS)]
        wsum = [at(f"wsum{b}", [P, PAD + S], F32, PB0 + UP * b) for b in range(2)]
        wpool = at("wpool", [P, GROUPS * P], F32, PB0 + 2 * UP + 4 * S)
        hn = [at("hn0", [P, S], F32, PB0 + 2 * UP), at("hn1", [P, S], F32, PB0)]
        names = ("q_hi", "q_lo", "k_hi", "k_lo")
        qh, ql, kh, kl = ([at(f"{n}{b}", [P, S], F32R, PB0 + 16 * KB * b + 4 * KB * j) for b in range(2)]
                          for j, n in enumerate(names))
        T1, T2 = R1 + 16 * KB, R1 + 48 * KB
        soft = [at(f"soft{b}", [P, HALF], F32, T1 + 2 * KB * b) for b in range(3)]
        loss = [at(f"loss{b}", [P, HALF], F32, T1 + 2 * KB * (3 + b)) for b in range(3)]
        later = [at(f"later{b}", [P, HALF], F32, T1 + 2 * KB * (6 + b)) for b in range(2)]
        loss_hi = [at(f"loss_hi{b}", [P, HALF], F32R, W0 + 8 * KB + 2 * KB * b) for b in range(4)]
        loss_lo = [at(f"loss_lo{b}", [P, HALF], F32R, W0 + 16 * KB + 2 * KB * b) for b in range(4)]
        attn = [at(f"attn{b}", [P, HALF], F32, T2 + 2 * KB * b) for b in range(4)]
        vp = [at(f"v_pair{b}", [P, SB, P], F32, T2 + 8 * KB + 4 * KB * b) for b in range(2)]
        on = [at(f"on{b}", [P, S], F32, PB0 + 4 * KB * b) for b in range(2)]
        osq = [at(f"osq{b}", [P, S], F32, PB0 + 8 * KB + 4 * KB * b) for b in range(NPAIR)]
        sq2 = [at(f"sq2{b}", [P, S], F32, PB0 + 20 * KB + 4 * KB * b) for b in range(2)]
        t2 = [at(f"t2{b}", [P, S], F32, PB0 + 4 * KB * b) for b in range(2)]
        ff_hi = at("ff_hi", [P, 2, S], F32R, KQ0)
        ff_lo = at("ff_lo", [P, 2, S], F32R, KQ0 + 8 * KB)
        wd_hi = at("wd_hi", [P, 2, D], F32R, KQ0 + 16 * KB)
        wd_lo = at("wd_lo", [P, 2, D], F32R, KQ0 + 24 * KB)
        wd_raw = at("wd_raw", [P, 2, D], F32, V0)
        cgate = [at(f"cgate{b}", [P, S], F32, PB0 + 8 * KB + 4 * KB * b) for b in range(2)]
        cval = [at("cval0", [P, S], F32, V0 + 8 * KB), at("cval1", [P, S], F32, V0 + 12 * KB)]
        silu = [at(f"silu{b}", [P, S], F32, PB0 + 16 * KB + 4 * KB * b) for b in range(2)]
        o_sb = [at(f"o_sb{b}", [P, SB, P], F32, PB0 + 24 * KB + 4 * KB * b) for b in range(2)]

        cst = small("cst", C_MASK)
        maskf = at("maskf", [P, P], F32, R1 + 4 * KB)
        negones, ones = small("negones", P), small("ones", P)
        tri = small("tri", P, F32R)
        ident_b, mask_b = small("ident_b", P, BF16), small("mask_b", P, BF16)
        acc = small("ada_acc", 512)
        one = small("one", 1)
        c_raw, c_act = small("c_raw", KT), small("c_act", KT)
        NPAR = 48 + 2 * KT + 2 * GROUPS + NPAIR + 2
        pcol = small("pcol", NPAR + 8 * FT)
        modc = small("modc", 48)
        gain = small("gain", 2 * KT)
        qg8 = small("qg8", 1)
        cpar = small("cpar", 16)
        assert place[0] <= 229368, place[0]

        ident, tri_f32 = cst[:, C_IDENT:C_TRI], cst[:, C_TRI:C_HEADAVG]
        headavg, ramp = cst[:, C_HEADAVG:C_RAMP], cst[:, C_RAMP:C_MASK]
        p_n1, p_n2 = 48, 48 + KT
        p_pb = p_n2 + KT
        p_ps, p_og = p_pb + GROUPS, p_pb + 2 * GROUPS
        p_qg = p_og + NPAIR
        p_kg = p_qg + 1
        m_sc1, m_sh1, m_g1, m_sh2, m_sc2, m_g2 = (KT * v for v in range(6))

        ps = ctx.enter_context(nc.psum_tensor("ps", [P, 8, HALF], F32))

        def sem(name):
            return ctx.enter_context(nc.semaphore(name))

        s_const, s_rows, s_c, s_poolw = sem("const_in"), sem("rows_in"), sem("c_in"), sem("poolw_in")
        s_x = [sem(f"x_in{h}") for h in range(2)]
        s_ada = [sem(f"ada_in{s}") for s in range(8)]
        s_w = [sem(f"w_in{b}") for b in range(2)]
        s_wd = sem("wd_in")
        s_fill = sem("fills_done")
        s_rowsT = sem("rows_turned")
        s_pcol = sem("params_ready")
        s_cact = sem("c_act_ready")
        s_acc, s_col = sem("ada_acc_ready"), sem("ada_cols_done")
        s_mod = sem("mod_ready")
        s_xps, s_sqx, s_ssum = sem("xT_in_psum"), sem("sqx_ready"), sem("ssum_added")
        s_ms, s_msread, s_rstd = sem("meansq_ready"), sem("meansq_read"), sem("rstd_ready")
        s_t, s_ahi, s_act = sem("normed_ready"), sem("act_hi_ready"), sem("act_ready")
        s_whi, s_wlo = sem("w_hi_ready"), sem("w_split_ready")
        s_tile, s_free = sem("tile_done"), sem("proj_consumed")
        s_sq = sem("headsq_ready")
        s_vps, s_v = sem("v_turned"), sem("v_tok_ready")
        s_pads, s_pooled, s_y, s_yev = sem("pads_zero"), sem("pooled_ready"), sem("y_in_psum"), sem("y_evacuated")
        s_mixhi, s_mix, s_mixv = sem("mix_hi_ready"), sem("mix_ready"), sem("mix_ready_by_vector")
        s_phi, s_pair, s_pairk = sem("pair_hi_ready"), sem("pair_q_ready"), sem("pair_k_ready")
        s_vp = sem("v_pair_ready")
        s_z, s_abs, s_ln, s_l = sem("z_ready"), sem("abs_ready"), sem("softlog_ready"), sem("loss_ready")
        s_lhi, s_llo = sem("loss_hi_ready"), [sem("loss_lo_even"), sem("loss_lo_odd")]
        s_r = sem("later_ready")
        s_e, s_a, s_av = sem("exponent_ready"), sem("attn_ready"), sem("attn_used")
        s_ofree = sem("o_evacuated")
        s_osq, s_on = sem("osq_ready"), sem("o_normed")
        s_sq2 = sem("sq2_ready")
        s_cpar = sem("conv_params_ready")
        s_cg, s_conv1, s_conv = sem("conv_base_ready"), sem("conv_first_tap"), sem("conv_ready")
        s_silu = sem("silu_ready")
        s_full, s_ffhi, s_ff = sem("ff_product_ready"), sem("ff_hi_ready"), sem("ff_ready")
        s_fflast = sem("last_ff_ready")
        s_wdhi, s_wds = sem("wd_hi_ready"), sem("wd_split_ready")
        s_down, s_dev = sem("down_done"), sem("down_evacuated")
        s_tout, s_oev = sem("out_turned"), sem("out_evacuated")
        s_out = [sem(f"out_stored{b}") for b in range(2)]
        s_dve, s_actc = sem("dve_chain"), sem("act_chain")

        w_in_v = w_in[0].rearrange("(k p) e -> p k e", p=P)
        w_out_v = w_out[0].rearrange("(k p) e -> p k e", p=P)
        w_up_v = w_up[0].rearrange("(k p) e -> p k e", p=P)
        w_dn_v = w_down[0].rearrange("(k p) e -> p k e", p=P)
        ada_v = ada_w[0].rearrange("(p k) n -> p k n", k=KT)

        def banks(n):
            return ps[:, 2 * (n % 2):2 * (n % 2) + 2, :]

        def flat(ap):
            return ap.rearrange("p a b -> p (a b)")

        ms_ps = flat(ps[:, 4:6, :])
        block = ctx.enter_context(nc.Block())

        @block.sync
        def _(sp):
            def load_x(h):
                sp.dma_start(x_tok[:, 4 * h:4 * h + 4, :],
                             x[0, HALF * h:HALF * h + HALF, :].rearrange("(j p) d -> p j d", p=P)).then_inc(s_x[h], 16)

            def load_first(pc):
                lo = D + 256 * pc if pc < 4 else 256 * (pc - 4)
                sp.dma_start(ada_piece[pc][:, :, :], ada_v[:, :, lo:lo + 256]).then_inc(s_ada[pc], 16)

            sp.dma_start(cst[:, :], consts[:, 0:C_MASK]).then_inc(s_const, 16)
            sp.dma_start(c_raw[:, :], c.rearrange("b (p k) -> (b p) k", k=KT)).then_inc(s_c, 16)
            load_x(0)
            load_first(0)
            load_x(1)
            load_first(1)
            rows = [(ada_b[0], 0, 48), (norm1_g[0], p_n1, KT), (norm2_g[0], p_n2, KT),
                    (pool_b[0].rearrange("g d -> (g d)"), p_pb, GROUPS), (pool_scale[0], p_ps, GROUPS),
                    (attn_out_g[0].rearrange("h d -> (h d)"), p_og, NPAIR)]
            for src, r, n in rows:
                sp.dma_start(prow[r:r + n, 0, :], src.rearrange("(r f) -> r f", f=P)).then_inc(s_rows, 16)
            for g, r in ((q_norm_g, p_qg), (k_norm_g, p_kg)):
                for h in range(2):
                    sp.dma_start(prow[r:r + 1, 0, 64 * h:64 * h + 64], g).then_inc(s_rows, 16)
            cw = conv_w[0].rearrange("j (m f) -> (j m) f", f=P)
            cb = conv_b[0].rearrange("(m f) -> m f", f=P)
            sp.dma_start(prow[0:4 * FT, 1, :], cw[0:4 * FT, :]).then_inc(s_rows, 16)
            sp.dma_start(prow[0:2 * FT, 2, :], cw[4 * FT:6 * FT, :]).then_inc(s_rows, 16)
            sp.dma_start(prow[2 * FT:4 * FT, 2, :], cb).then_inc(s_rows, 16)
            sp.dma_start(maskf[:, :], consts[:, C_MASK:C_END]).then_inc(s_const, 16)
            for pc in range(2, 8):
                load_first(pc)
            for n in range(2):
                sp.dma_start(w_raw[n][:, :, :], w_in_v[:, :, P * n:P * n + P]).then_inc(s_w[n], 16)

            def load_piece(pc, parity):
                sp.wait_ge(s_acc, 2 * pc - 2)
                sp.dma_start(ada_piece[4 + parity][:, :, :],
                             ada_v[:, :, ds(pc * 256, 256)]).then_inc(s_ada[4 + parity], 16)

            def load_tile(n, parity, src, col):
                sp.wait_ge(s_wlo, n - 1)
                sp.dma_start(w_raw[parity][:, :, :], src[:, :, ds(col, P)]).then_inc(s_w[parity], 16)

            for n in range(2, 4):
                load_tile(n, n % 2, w_in_v, n * P)
            sp.wait_ge(s_acc, 16)
            sp.dma_start(wpool[:, :].rearrange("p (g d) -> p g d", g=GROUPS),
                         pool_w[0].rearrange("g c d -> c g d")).then_inc(s_poolw, 16)
            load_piece(8, 0)
            load_piece(9, 1)
            for n in range(4, T_Q + 4):
                load_tile(n, n % 2, w_in_v, n * P)
            with sp.Fori(0, NPAIR - 1) as j:
                for b in range(2):
                    load_tile(2 * j + (T_Q + 4 + b), b, w_in_v, (2 * j + (T_Q + 4 + b)) * P)
                    load_piece(4 * j + (10 + 2 * b), 0)
                    load_piece(4 * j + (11 + 2 * b), 1)
            load_tile(N_IN - 2, 0, w_in_v, (N_IN - 2) * P)
            load_piece(22, 0)
            load_piece(23, 1)
            load_tile(N_IN - 1, 1, w_in_v, (N_IN - 1) * P)
            with sp.Fori(0, KT // 2) as j:
                for b in range(2):
                    load_tile(2 * j + (T_OUT + b), b, w_out_v, (2 * j + b) * P)
            for b in range(2):
                load_tile(T_UP + b, b, w_up_v, b * DFF)
            sp.wait_ge(s_on, NPAIR)
            sp.dma_start(wd_raw[:, :, :], w_dn_v[:, 0:2, :]).then_inc(s_wd, 16)

            with sp.Fori(0, NG - 1) as g:
                load_tile(4 * g + (T_UP + 2), 0, w_up_v, (2 * g + 1) * P)
                load_tile(4 * g + (T_UP + 3), 1, w_up_v, (2 * g + 1) * P + DFF)
                load_tile(4 * g + (T_UP + 4), 0, w_up_v, (2 * g + 2) * P)
                load_tile(4 * g + (T_UP + 5), 1, w_up_v, (2 * g + 2) * P + DFF)
                sp.wait_ge(s_wds, g + 1)
                sp.dma_start(wd_raw[:, :, :], w_dn_v[:, ds(2 * g + 2, 2), :]).then_inc(s_wd, 16)
            load_tile(T_UP + 4 * NG - 2, 0, w_up_v, (FT - 1) * P)
            load_tile(T_UP + 4 * NG - 1, 1, w_up_v, (FT - 1) * P + DFF)
            for m in range(KT):
                sp.wait_ge(s_oev, m + 1)
                sp.dma_start(out[0].rearrange("(j p) d -> p j d", p=P)[:, :, P * m:P * m + P],
                             o_sb[m % 2][:, :, :]).then_inc(s_out[m % 2], 16)
            for b in range(2):
                sp.wait_ge(s_out[b], 16 * (KT // 2))

        @block.gpsimd
        def _(pool):
            g_ = nc.gpsimd

            g_.memset(negones[:, :], -1.0).then_inc(s_fill, 1)
            g_.memset(ones[:, :], 1.0).then_inc(s_fill, 1)
            g_.memset(one[:, :], 1.0).then_inc(s_fill, 1)

            def low_part(n, b):
                pool.wait_ge(s_whi, n + 1)
                g_.tensor_tensor(w_lo[b][:, :, :], w_raw[b][:, :, :], w_hi[b][:, :, :].bitcast(F32),
                                 ALU.subtract).then_inc(s_wlo, 1)

            for h in range(2):
                for k in range(1, KT):
                    u = h * KT + k
                    pool.wait_ge(s_sqx, u + 1)
                    if k > 1:
                        pool.wait_ge(s_ssum, h * (KT - 1) + k - 1)
                    cols = slice(HALF * h, HALF * h + HALF)
                    g_.tensor_tensor(ssum[:, cols], ssum[:, cols], sqx[u % 2][:, :], ALU.add).then_inc(s_ssum, 1)
            low_part(0, 0)
            low_part(1, 1)
            pool.wait_ge(s_act, KT)
            for t in (*u_pad, *wsum):
                g_.memset(t[:, 0:PAD], 0.0).then_inc(s_pads, 1)
            for n in range(2, N_IN):
                low_part(n, n % 2)
            def q_low(b, q, count):
                pool.wait_ge(s_phi, count)
                g_.tensor_tensor(ql[b][:, :], kq_f[:, ds(q * S, S)], qh[b][:, :].bitcast(F32),
                                 ALU.subtract).then_inc(s_pair, 1)

            q_low(0, 0, 1)
            for g in range(2):
                pool.wait_ge(s_mixhi, g + 1)
                g_.tensor_tensor(act_lo[:, g, :], u_pad[g][:, PAD:], act_hi[:, g, :].bitcast(F32),
                                 ALU.subtract).then_inc(s_mix, 1)

            with pool.Fori(0, NPAIR // 2) as it:
                for n in range(NB):
                    par, h, i = BODY[n]
                    if n == SECOND + 2:
                        q_low(1, 2 * it + 1, 4 * it + 3)
                    if n == NEXT + 2:
                        q_low(0, it + 2, 4 * it + 5)
                    cols = slice(col0(n), HALF)
                    if n % 2:
                        pool.wait_ge(s_lhi, it * NB + n + 1)
                        g_.tensor_tensor(loss_lo[n % 4][:, cols], loss[n % 3][:, cols],
                                         loss_hi[n % 4][:, cols].bitcast(F32), ALU.subtract).then_inc(s_llo[1], 1)
                    if i == 0:
                        continue
                    pool.wait_ge(s_l, it * NB + n + 1)
                    if n:
                        pool.wait_ge(s_e, it * NB + n)
                    new, old = col0(n), HALF
                    if i != 4 * h + 3:
                        pool.wait_ge(s_r, it * ADDS_BEFORE[NB] + ADDS_BEFORE[n])
                        old = col0(n - 1)
                        ins = g_.tensor_tensor(later[(n + 1) % 2][:, old:HALF], later[n % 2][:, old:HALF],
                                               loss[n % 3][:, old:HALF], ALU.subtract)
                    if new < old:
                        ins = g_.tensor_tensor(later[(n + 1) % 2][:, new:old], loss[n % 3][:, new:old],
                                               negones[:, 0:old - new], ALU.mult)
                    ins.then_inc(s_r, 1)

            low_part(T_OUT, 0)
            for m in range(KT):
                low_part(T_OUT + m + 2, m % 2)
                if 0 < m < KT - 1:
                    pool.wait_ge(s_sq2, m + 1)
                    if m > 1:
                        pool.wait_ge(s_ssum, 2 * (KT - 1) + m - 1)
                    g_.tensor_tensor(ssum[:, :], ssum[:, :], sq2[m % 2][:, :], ALU.add).then_inc(s_ssum, 1)

            def group(g, last):
                n = 4 * g + T_UP
                low_part(n + 2, 0)
                low_part(n + 3, 1)
                low_ff(2 * g, 0)
                pool.wait_ge(s_wdhi, g + 1)
                g_.tensor_tensor(wd_lo[:, :, :], wd_raw[:, :, :], wd_hi[:, :, :].bitcast(F32),
                                 ALU.subtract).then_inc(s_wds, 1)
                if not last:
                    low_part(n + 4, 0)
                    low_part(n + 5, 1)
                    low_ff(2 * g + 1, 1)

            def low_ff(f, b):
                pool.wait_ge(s_ffhi, f + 1)
                g_.tensor_tensor(ff_lo[:, b, :], cval[b][:, :], ff_hi[:, b, :].bitcast(F32),
                                 ALU.subtract).then_inc(s_ff, 1)

            with pool.Fori(0, NG - 1) as g:
                group(g, False)
            group(NG - 1, True)

        @block.scalar
        def _(act):
            a_ = nc.scalar

            def high_part(n, b, count):
                act.wait_ge(s_w[b], 16 * count)
                a_.activation(w_hi[b][:, :, :], w_raw[b][:, :, :], ACT.Identity).then_inc(s_whi, 1)

            def rstd(dst, src, r, scale=1.0):
                act.wait_ge(s_ms, r + 1)
                a_.activation(dst, src, ACT.Ln, bias=EPS, scale=scale).then_inc(s_msread, 1)
                act.wait_ge(s_msread, r + 1)
                a_.activation(dst, dst, ACT.Exp, scale=-0.5).then_inc(s_rstd, 1)

            act.wait_ge(s_c, 16)
            a_.activation(c_act[:, :], c_raw[:, :], ACT.Silu).then_inc(s_cact, 1)
            act.preload_act_table_set("natural_log_exp_and_others")
            for h in range(2):
                for k in range(KT):
                    u = h * KT + k
                    act.wait_ge(s_xps, u + 1)
                    a_.activation(xT[:, k, HALF * h:HALF * h + HALF], ps[:, u % 4, :], ACT.Identity)
                    last = max((q for q in range(u) if k and q % KT and q % 2 == u % 2), default=0)
                    if last:
                        act.wait_ge(s_ssum, last - last // KT)
                    dst = ssum[:, HALF * h:HALF * h + HALF] if k == 0 else sqx[u % 2][:, :]
                    a_.activation(dst, ps[:, u % 4, :], ACT.Square).then_inc(s_sqx, 1)
            high_part(0, 0, 1)
            high_part(1, 1, 1)
            rstd(ssum[:, :], ms_ps, 0, 1.0 / D)
            for k in range(KT):
                act.wait_ge(s_t, k + 1)
                a_.activation(act_hi[:, k, :], tnorm[k % 2][:, :], ACT.Identity,
                              bias=modc[:, m_sh1 + k:m_sh1 + k + 1]).then_inc(s_ahi, 1)
            for i in range(N_IN):
                act.wait_ge(s_tile, i + 1)
                r = i - T_Q
                if T_Q <= i < T_V:
                    if i == T_Q + 1:
                        act.wait_ge(s_pooled, GROUPS)
                    if r >= 2:
                        act.wait_ge(s_free, i - 1)
                    a_.activation(hn[r % 2][:, :], flat(banks(i)), ACT.Square).then_inc(s_sq, 1)
                if i + 2 < N_IN:
                    high_part(i + 2, i % 2, i // 2 + 2)
                if T_Q <= i < T_V:
                    rstd(hn[r % 2][:, :], ms_ps, 1 + r)
            act.wait_ge(s_yev, GROUPS)
            for g in range(GROUPS):
                a_.activation(act_hi[:, g, :], u_pad[g][:, PAD:], ACT.Identity).then_inc(s_mixhi, 1)

            with act.Fori(0, NPAIR // 2) as it:
                def weights(n):
                    act.wait_ge(s_e, it * NB + n + 1)
                    if n >= 4:
                        act.wait_ge(s_av, it * NB + n - 3)
                    cols = slice(col0(n), HALF)
                    a_.activation(attn[n % 4][:, cols], ps[:, n % 6, cols], ACT.Exp).then_inc(s_a, 1)

                for n in range(NB):
                    cols = slice(col0(n), HALF)
                    act.wait_ge(s_abs, it * NB + n + 1)
                    a_.activation(soft[n % 3][:, cols], soft[n % 3][:, cols], ACT.Exp, scale=-1.0).then_inc(s_actc, 1)
                    if n >= 4:
                        weights(n - 4)
                    act.wait_ge(s_actc, it * NB + n + 1)
                    a_.activation(soft[n % 3][:, cols], soft[n % 3][:, cols], ACT.Ln, bias=1.0).then_inc(s_ln, 1)
                for n in range(NB - 4, NB):
                    weights(n)

            for b in range(2):
                high_part(T_OUT + b, b, T_OUT // 2 + 1)
            act.wait_ge(s_ofree, 4 * NPAIR)
            for p in range(NPAIR):
                a_.activation(osq[p][:, :], kq[:, NPAIR + p, :], ACT.Square).then_inc(s_osq, 1)
            for p in range(NPAIR + 1):
                if p < NPAIR:
                    rstd(osq[p][:, :], flat(ps[:, 4 + 2 * (p % 2):6 + 2 * (p % 2), :]), 1 + 2 * NPAIR + p)
                if p:
                    act.wait_ge(s_on, p)
                    a_.activation(act_hi[:, NPAIR + p - 1, :], on[(p - 1) % 2][:, :], ACT.Identity).then_inc(s_ahi, 1)
            for m in range(KT):
                n = T_OUT + m
                act.wait_ge(s_tile, n + 1)
                high_part(n + 2, n % 2, n // 2 + 2)
                act.wait_ge(s_free, n + 1)
                if m >= 3:
                    act.wait_ge(s_ssum, 2 * (KT - 1) + m - 2)
                a_.activation(ssum[:, :] if m == 0 else sq2[m % 2][:, :], xT[:, m, :], ACT.Square).then_inc(s_sq2, 1)
            rstd(ssum[:, :], ms_ps, 1 + 3 * NPAIR, 1.0 / D)
            for k in range(KT):
                act.wait_ge(s_t, KT + k + 1)
                a_.activation(act_hi[:, k, :], t2[k % 2][:, :], ACT.Identity,
                              bias=modc[:, m_sh2 + k:m_sh2 + k + 1]).then_inc(s_ahi, 1)

            act.preload_act_table_set("silu_and_others")

            def group(g, last, first):
                n0 = 4 * g + T_UP
                act.wait_ge(s_cpar, g + 1)
                for b in range(2):
                    f = 2 * g + b
                    for half, dst in ((0, cgate), (1, cval)):
                        n = n0 + (2 * b + half)
                        act.wait_ge(s_tile, n + 1)
                        if half and not first:
                            act.wait_ge(s_ff, f - 1)
                        v = cpar[:, :].rearrange("p (j h b) -> p j h b", j=4, h=2)
                        a_.activation(dst[b][:, :], flat(banks(half)), ACT.Identity,
                                      scale=v[:, 2, half, b:b + 1], bias=v[:, 3, half, b:b + 1]).then_inc(s_cg, 1)
                        if not (last and b == 1):
                            high_part(n + 2, half, 2 * g + ((T_UP + 2 * b) // 2 + 2))
                    act.wait_ge(s_conv, 2 * f + 1)
                    if not first:
                        act.wait_ge(s_full, f - 1)
                    a_.activation(silu[b][:, :], cgate[b][:, :], ACT.Silu).then_inc(s_silu, 1)
                    act.wait_ge(s_full, f + 1)
                    if not first and b == 0:
                        act.wait_ge(s_down, 8 * g)
                    a_.activation(ff_hi[:, b, :], cval[b][:, :], ACT.Identity).then_inc(s_ffhi, 1)
                    if b == 0:
                        act.wait_ge(s_wd, 16 * g + 16)
                        a_.activation(wd_hi[:, :, :], wd_raw[:, :, :], ACT.Identity).then_inc(s_wdhi, 1)

            group(0, False, True)
            with act.Fori(1, NG - 1) as g:
                group(g, False, False)
            group(NG - 1, True, False)
            for m in range(KT):
                act.wait_ge(s_tout, m + 1)
                if m >= 2:
                    act.wait_ge(s_out[m % 2], 16 * (m // 2))
                a_.activation(o_sb[m % 2][:, :, :].rearrange("p j d -> p (j d)"), flat(banks(m)),
                              ACT.Identity).then_inc(s_oev, 1)

        @block.vector
        def _(dve):
            v_ = nc.vector
            done = [0]

            def link(ins):
                done[0] += 1
                ins.then_inc(s_dve, 1)
                dve.wait_ge(s_dve, done[0])

            def parameters():
                dve.wait_ge(s_const, 32)
                v_.tensor_copy(ident_b[:, :], ident).then_inc(s_pcol, 1)
                v_.tensor_copy(mask_b[:, :], maskf[:, :]).then_inc(s_pcol, 1)
                v_.tensor_copy(tri[:, :], tri_f32).then_inc(s_pcol, 1)
                dve.wait_ge(s_rowsT, 1)
                link(v_.tensor_copy(pcol[:, :], ps[:, 7, 0:NPAR + 8 * FT]))
                v_.tensor_scalar(qg8[:, :], pcol[:, p_qg:p_qg + 1], 0.125, None, ALU.mult).then_inc(s_pcol, 1)

            dve.wait_ge(s_cact, 1)

            def piece(pc, slot, count):
                dve.wait_ge(s_ada[slot], 16 * count)
                dst = acc_first[pc % 2] if pc < 8 else acc
                free = pc - 1 if pc < 8 else pc
                if free > 0:
                    dve.wait_ge(s_col, free)
                    dve.wait_ge(s_acc, 2 * free)
                src = ada_piece[slot]
                for k in range(KT):
                    half = dst[:, 256 * (k % 2):256 * (k % 2) + 256]
                    if k < 2:
                        ins = v_.tensor_scalar(half, src[:, k, :], c_act[:, k:k + 1], None, ALU.mult)
                    else:
                        dve.wait_ge(s_dve, done[0] - (k < KT - 1))
                        ins = v_.scalar_tensor_tensor(out=half, in0=src[:, k, :], scalar=c_act[:, k:k + 1],
                                                      in1=half, op0=ALU.mult, op1=ALU.add)
                    if k < KT - 2:
                        ins.then_inc(s_dve, 1)
                        done[0] += 1
                    else:
                        ins.then_inc(s_acc, 1)

            for pc in range(8):
                piece(pc, pc, 1)
                if pc == 5:
                    parameters()
            dve.wait_ge(s_col, 8)
            link(v_.tensor_tensor(modc[:, m_sc1:m_sc1 + KT], ps[:, 6, 0:KT], pcol[:, KT:2 * KT], ALU.add))
            v_.tensor_tensor(modc[:, m_sh1:m_sh1 + KT], ps[:, 6, KT:2 * KT], pcol[:, 0:KT], ALU.add).then_inc(s_mod, 1)
            link(v_.scalar_tensor_tensor(out=gain[:, 0:KT], in0=modc[:, m_sc1:m_sc1 + KT], scalar=1.0,
                                         in1=pcol[:, p_n1:p_n1 + KT], op0=ALU.add, op1=ALU.mult))
            dve.wait_ge(s_mod, 1)

            def norm(tmp, gcol, shift, r, base, before):
                dve.wait_ge(s_rstd, r + 1)
                for k in range(KT + 1):
                    if k >= 2:
                        dve.wait_ge(s_act, before + k - 1)
                    if k < KT:
                        v_.scalar_tensor_tensor(out=tmp[k % 2][:, :], in0=xT[:, k, :],
                                                scalar=gain[:, gcol + k:gcol + k + 1], in1=ssum[:, :],
                                                op0=ALU.mult, op1=ALU.mult).then_inc(s_t, 1)
                    if k:
                        q = k - 1
                        dve.wait_ge(s_ahi, base + q + 1)
                        v_.scalar_tensor_tensor(out=act_lo[:, q, :], in0=tmp[q % 2][:, :],
                                                scalar=modc[:, shift + q:shift + q + 1],
                                                in1=act_hi[:, q, :].bitcast(F32), op0=ALU.add,
                                                op1=ALU.subtract).then_inc(s_act, 1)

            norm(tnorm, 0, m_sh1, 0, 0, 0)

            def pooled_output(g):
                dve.wait_ge(s_y, g + 1)
                v_.tensor_scalar(u_pad[g][:, PAD:], flat(ps[:, 6:8, :]), pcol[:, p_pb + g:p_pb + g + 1],
                                 pcol[:, p_ps + g:p_ps + g + 1], ALU.add, ALU.mult).then_inc(s_yev, 1)

            for i in range(N_IN):
                r = i - T_Q
                if 0 <= r < 2 * NPAIR:
                    piece(8 + 2 * r, 4, r + 2)
                dve.wait_ge(s_tile, i + 1)
                if i < T_Q:
                    g, w = i, POOL_WINDOWS[i]
                    if i == 0:
                        dve.wait_ge(s_pads, 6)
                    v_.tensor_copy(u_pad[g][:, PAD:], flat(banks(i))).then_inc(s_free, 1)
                    dve.wait_ge(s_free, i + 1)
                    cur, step, b = u_pad[g], 1, 0
                    while step < w:
                        link(v_.tensor_tensor(wsum[b][:, PAD:], cur[:, PAD:], cur[:, PAD - step:PAD + S - step],
                                              ALU.add))
                        cur, step, b = wsum[b], 2 * step, 1 - b
                    link(v_.scalar_tensor_tensor(out=cur[:, PAD:PAD + w], in0=cur[:, PAD:PAD + w], scalar=w / PAD,
                                                 in1=ramp[:, 0:w], op0=ALU.mult, op1=ALU.mult))
                    v_.scalar_tensor_tensor(out=u_pad[g][:, PAD:], in0=cur[:, PAD:], scalar=1.0 / w,
                                            in1=u_pad[g][:, PAD:], op0=ALU.mult, op1=ALU.subtract).then_inc(s_pooled, 1)
                    if i:
                        pooled_output(i - 1)
                    if i == T_Q - 1:
                        pooled_output(i)
                elif i < T_V:
                    dve.wait_ge(s_rstd, r + 2)
                    g = qg8[:, :] if i < T_K else pcol[:, p_kg:p_kg + 1]
                    v_.scalar_tensor_tensor(out=kq[:, r, :], in0=flat(banks(i)), scalar=g, in1=hn[r % 2][:, :],
                                            op0=ALU.mult, op1=ALU.mult).then_inc(s_free, 1)
                    piece(9 + 2 * r, 5, r + 2)
                    if i == T_V - 1:
                        dve.wait_ge(s_col, 24)
                        v_.tensor_tensor(modc[:, 2 * KT:6 * KT], ps[:, 6, 2 * KT:6 * KT], pcol[:, 2 * KT:6 * KT],
                                         ALU.add).then_inc(s_mod, 1)
                        dve.wait_ge(s_mod, 2)
                        link(v_.scalar_tensor_tensor(out=gain[:, KT:2 * KT], in0=modc[:, m_sc2:m_sc2 + KT], scalar=1.0,
                                                     in1=pcol[:, p_n2:p_n2 + KT], op0=ALU.add, op1=ALU.mult))
                else:
                    q = i - T_V
                    if q >= 2:
                        dve.wait_ge(s_vps, q - 1)
                    v_.tensor_copy(hn[q % 2][:, :], flat(banks(i))).then_inc(s_free, 1)
                    dve.wait_ge(s_vps, q + 1)
                    v_.tensor_copy(v_tok[:, :, P * q:P * q + P],
                                   ms_ps.rearrange("p (j d) -> p j d", j=SB)).then_inc(s_v, 1)
            dve.wait_ge(s_v, NPAIR)
            dve.wait_ge(s_free, N_IN)

            def split_pair(step, b, pair, count):
                k = kq_f[:, ds((pair + NPAIR) * S, S)]
                if step == 0:
                    v_.tensor_scalar(qh[b][:, :], kq_f[:, ds(pair * S, S)], 1.0, None, ALU.mult).then_inc(s_phi, 1)
                elif step == 1:
                    v_.tensor_scalar(kh[b][:, :], k, 1.0, None, ALU.mult).then_inc(s_phi, 1)
                elif step == 2:
                    dve.wait_ge(s_phi, count + 2)
                    v_.tensor_tensor(kl[b][:, :], k, kh[b][:, :].bitcast(F32), ALU.subtract).then_inc(s_pairk, 1)
                else:
                    v_.tensor_scalar(vp[b][:, :, :], v_tok[:, :, ds(pair * P, P)], 1.0, None,
                                     ALU.mult).then_inc(s_vp, 1)

            for step in range(4):
                split_pair(step, 0, 0, 0)
            for g in range(2, GROUPS):
                dve.wait_ge(s_mixhi, g + 1)
                v_.tensor_tensor(act_lo[:, g, :], u_pad[g][:, PAD:], act_hi[:, g, :].bitcast(F32),
                                 ALU.subtract).then_inc(s_mixv, 1)

            with dve.Fori(0, NPAIR // 2) as it:
                def losses(n):
                    cols = slice(col0(n), HALF)
                    dve.wait_ge(s_ln, it * NB + n + 1)
                    if n >= 3:
                        dve.wait_ge(s_llo[(n - 3) % 2], it * (NB // 2) + (n - 3) // 2 + 1)
                        if ADDS_BEFORE[n - 2]:
                            dve.wait_ge(s_r, it * ADDS_BEFORE[NB] + ADDS_BEFORE[n - 2])
                    v_.scalar_tensor_tensor(out=loss[n % 3][:, cols], in0=ps[:, n % 6, cols], scalar=0.0,
                                            in1=soft[n % 3][:, cols], op0=ALU.max, op1=ALU.add).then_inc(s_l, 1)

                def loss_high(n):
                    cols = slice(col0(n), HALF)
                    dve.wait_ge(s_l, it * NB + n + 1)
                    if n >= 4:
                        dve.wait_ge(s_e, it * NB + n - 3)
                    v_.tensor_copy(loss_hi[n % 4][:, cols], loss[n % 3][:, cols]).then_inc(s_lhi, 1)

                def loss_low(n):
                    cols = slice(col0(n), HALF)
                    dve.wait_ge(s_lhi, it * NB + n + 1)
                    if n >= 4:
                        dve.wait_ge(s_e, it * NB + n - 3)
                    v_.tensor_tensor(loss_lo[n % 4][:, cols], loss[n % 3][:, cols],
                                     loss_hi[n % 4][:, cols].bitcast(F32), ALU.subtract).then_inc(s_llo[0], 1)

                def evacuate(s):
                    par, h, _ = BODY[LAST_OF[s]]
                    pair = s // (NSEQ // 2)
                    rows = slice(64 * par, 64 * par + 64)
                    if s == NSEQ // 2:
                        dve.wait_ge(s_pairk, 2 * it + 3)
                    dve.wait_ge(s_av, it * NB + LAST_OF[s] + 1)
                    v_.tensor_scalar(kq_f[rows, ds((2 * it + (NPAIR + pair)) * S + HALF * h, HALF)],
                                     ps[rows, 6 + s % 2, :], 1.0, None, ALU.mult).then_inc(s_ofree, 1)

                for n in range(NB + 2):
                    if n < NB:
                        cols = slice(col0(n), HALF)
                        dve.wait_ge(s_z, it * NB + n + 1)
                        if n >= 3:
                            dve.wait_ge(s_l, it * NB + n - 2)
                        v_.tensor_scalar(soft[n % 3][:, cols].bitcast(U32), ps[:, n % 6, cols].bitcast(U32), ABS_BITS,
                                         None, ALU.bitwise_and).then_inc(s_abs, 1)
                    if n >= 2:
                        loss_high(n - 2)
                    if 1 <= n <= NB:
                        losses(n - 1)
                    if n >= 2 and n % 2 == 0:
                        loss_low(n - 2)
                    if n == SECOND:
                        dve.wait_ge(s_mix, 2)
                        dve.wait_ge(s_mixv, 2)
                    if n in range(SECOND, SECOND + 8, 2):
                        split_pair((n - SECOND) // 2, 1, 2 * it + 1, 4 * it + 2)
                    if n == NEXT:
                        dve.wait_ge(s_av, it * NB + NU)
                        dve.wait_ge(s_ofree, NSEQ // 2)
                    if NEXT <= n < NEXT + 4:
                        split_pair(n - NEXT, 0, it + 2, 4 * it + 4)
                    for s in range(NSEQ):
                        if LAST_OF[s] + 6 == n:
                            evacuate(s)
                evacuate(NSEQ - 1)

            dve.wait_ge(s_whi, T_OUT + 2)
            dve.wait_ge(s_wlo, T_OUT + 1)
            v_.tensor_tensor(w_lo[1][:, :, :], w_raw[1][:, :, :], w_hi[1][:, :, :].bitcast(F32),
                             ALU.subtract).then_inc(s_wlo, 1)

            def head_low(p):
                dve.wait_ge(s_ahi, KT + p + 1)
                v_.tensor_tensor(act_lo[:, NPAIR + p, :], on[p % 2][:, :], act_hi[:, NPAIR + p, :].bitcast(F32),
                                 ALU.subtract).then_inc(s_mixv, 1)

            for p in range(NPAIR):
                dve.wait_ge(s_rstd, 2 + 2 * NPAIR + p)
                if p >= 2:
                    dve.wait_ge(s_mixv, p + 1)
                v_.scalar_tensor_tensor(out=on[p % 2][:, :], in0=kq[:, NPAIR + p, :],
                                        scalar=pcol[:, p_og + p:p_og + p + 1], in1=osq[p][:, :],
                                        op0=ALU.mult, op1=ALU.mult).then_inc(s_on, 1)
                if p:
                    head_low(p - 1)
            head_low(NPAIR - 1)
            for m in range(KT):
                dve.wait_ge(s_tile, T_OUT + m + 1)
                v_.scalar_tensor_tensor(out=xT[:, m, :], in0=flat(banks(m)), scalar=modc[:, m_g1 + m:m_g1 + m + 1],
                                        in1=xT[:, m, :], op0=ALU.mult, op1=ALU.add).then_inc(s_free, 1)
            dve.wait_ge(s_free, T_OUT + KT)
            norm(t2, KT, m_sh2, 1 + 3 * NPAIR, KT + NPAIR, KT)

            conv_v = pcol[:, NPAR:NPAR + 8 * FT].rearrange("p (j h f) -> p j h f", j=4, h=2)

            def group(g, first):
                if not first:
                    dve.wait_ge(s_cg, 4 * g)
                if not (isinstance(g, int) and g < 2):
                    dve.wait_ge(s_dev, 8 * g - 8)
                v_.tensor_scalar(cpar[:, :].rearrange("p (j h b) -> p j h b", j=4, h=2),
                                 conv_v[:, :, :, ds(2 * g, 2)], 1.0, None, ALU.mult).then_inc(s_cpar, 1)
                dve.wait_ge(s_cpar, g + 1)
                for b in range(2):
                    for half, dst in ((0, cgate), (1, cval)):
                        v = cpar[:, :].rearrange("p (j h b) -> p j h b", j=4, h=2)
                        r = 2 * b + half
                        src = flat(banks(half))
                        dve.wait_ge(s_cg, 4 * g + (r + 1))
                        v_.scalar_tensor_tensor(out=dst[b][:, 1:S], in0=src[:, 0:S - 1], scalar=v[:, 1, half, b:b + 1],
                                                in1=dst[b][:, 1:S], op0=ALU.mult, op1=ALU.add).then_inc(s_conv1, 1)
                        dve.wait_ge(s_conv1, 4 * g + (r + 1))
                        v_.scalar_tensor_tensor(out=dst[b][:, 2:S], in0=src[:, 0:S - 2], scalar=v[:, 0, half, b:b + 1],
                                                in1=dst[b][:, 2:S], op0=ALU.mult, op1=ALU.add).then_inc(s_conv, 1)
                    evacuates = b == 0 and not first
                    if evacuates:
                        evac_down(8 * g - 8, 0)
                    dve.wait_ge(s_conv, 4 * g + (2 * b + 2))
                    dve.wait_ge(s_silu, 2 * g + (b + 1))
                    v_.tensor_tensor(cval[b][:, :], cval[b][:, :], silu[b][:, :], ALU.mult).then_inc(s_full, 1)
                    if evacuates:
                        for m in range(1, KT):
                            evac_down(8 * g - 8, m)

            def evac_down(base, m):
                dve.wait_ge(s_down, base + (m + 1))
                v_.scalar_tensor_tensor(out=xT[:, m, :], in0=flat(ps[:, 4 + 2 * (m % 2):6 + 2 * (m % 2), :]),
                                        scalar=modc[:, m_g2 + m:m_g2 + m + 1], in1=xT[:, m, :], op0=ALU.mult,
                                        op1=ALU.add).then_inc(s_dev, 1)

            group(0, True)
            group(1, False)
            with dve.Fori(2, NG - 1) as g:
                group(g, False)
            group(NG - 1, False)
            dve.wait_ge(s_ffhi, FT)
            v_.tensor_tensor(ff_lo[:, 1, :], cval[1][:, :], ff_hi[:, 1, :].bitcast(F32),
                             ALU.subtract).then_inc(s_fflast, 1)
            dve.wait_ge(s_dev, 8 * NG - 8)
            for m in range(KT):
                evac_down(8 * NG - 8, m)

        @block.tensor
        def _(pe):
            t_ = nc.tensor

            def product(n, b, ks, moving_ready=None):
                for k in ks:
                    if moving_ready is not None:
                        pe.wait_ge(*moving_ready(k))
                    seq = [(w_hi, act_hi, 0), (w_hi, act_hi, 1), (w_hi, act_lo, 0), (w_hi, act_lo, 1),
                           (w_lo, act_hi, 0), (w_lo, act_hi, 1)]
                    for j, (w, a, h) in enumerate(seq):
                        mm = t_.matmul(ps[:, 2 * b + h, :], w[b][:, k, :], a[:, k, HALF * h:HALF * h + HALF],
                                       start=(k == 0 and j < 2), stop=(k == KT - 1 and j >= 4))
                return mm

            def begin(n):
                pe.wait_ge(s_wlo, n + 1)
                if not isinstance(n, int) or n >= 2:
                    pe.wait_ge(s_free, n - 1)

            def begin_up(n):
                pe.wait_ge(s_wlo, n + 1)
                pe.wait_ge(s_conv, n - (T_UP + 1))

            def tile(n, b, begin=begin):
                begin(n)
                product(n, b, range(KT)).then_inc(s_tile, 1)

            def two_tiles(ks, moving_ready):
                for k in ks:
                    m0 = product(0, 0, [k], moving_ready)
                    if k < KT - 2:
                        product(1, 1, [k])
                m0.then_inc(s_tile, 1)
                product(1, 1, range(KT - 2, KT)).then_inc(s_tile, 1)

            def ada_cols(pc, col, acc=acc):
                pe.wait_ge(s_acc, 2 * pc + 2)
                for h in range(2):
                    dst = ps[:, 6, col + h:col + h + 1] if isinstance(col, int) else ps[:, 6, ds(col + h, 1)]
                    for e in range(2):
                        mm = t_.matmul(dst, acc[:, 256 * e + P * h:256 * e + P * h + P], one[:, :],
                                       start=(e == 0), stop=(e == 1))
                mm.then_inc(s_col, 1)

            def means(weights, src, bank):
                for h in range(2):
                    mm = t_.matmul(ps[:, bank + h, :], weights, src[:, HALF * h:HALF * h + HALF], start=True, stop=True)
                mm.then_inc(s_ms, 1)

            def turn_x(h):
                pe.wait_ge(s_x[h], 16)
                for k in range(KT):
                    u = h * KT + k
                    if u >= 4:
                        pe.wait_ge(s_sqx, u - 3)
                    for j in range(4):
                        mm = t_.transpose(ps[:, u % 4, P * j:P * j + P], x_tok[:, 4 * h + j, P * k:P * k + P], ident)
                    mm.then_inc(s_xps, 1)

            pe.wait_ge(s_const, 16)
            turn_x(0)
            turn_x(1)
            pe.wait_ge(s_rows, 16 * 13)
            for j, (r, lo) in enumerate(((NPAR, 0), (4 * FT, NPAR), (4 * FT, NPAR + 4 * FT))):
                mm = t_.transpose(ps[:, 7, lo:lo + r], prow[0:r, j, :], ident[0:r, 0:r])
            mm.then_inc(s_rowsT, 1)
            pe.wait_ge(s_fill, 3)
            for pc in range(4):
                ada_cols(pc, 2 * pc, acc_first[pc % 2])
            pe.wait_ge(s_ssum, 2 * (KT - 1))
            means(ones[:, :], ssum, 4)
            for pc in range(4, 8):
                ada_cols(pc, 2 * pc, acc_first[pc % 2])

            begin(0)
            begin(1)
            two_tiles(range(KT), lambda k: (s_act, k + 1))

            def group_map(g):
                pe.wait_ge(s_pooled, g + 1)
                if g:
                    pe.wait_ge(s_yev, g)
                for h in range(2):
                    mm = t_.matmul(ps[:, 6 + h, :], wpool[:, P * g:P * g + P],
                                   u_pad[g][:, PAD + HALF * h:PAD + HALF * h + HALF], start=True, stop=True)
                mm.then_inc(s_y, 1)

            pe.wait_ge(s_mod, 1)
            pe.wait_ge(s_poolw, 16)
            for n in range(2, T_Q + 1):
                begin(n)
                product(n, n % 2, range(0, 4))
                group_map(n - 2)
                product(n, n % 2, range(4, KT)).then_inc(s_tile, 1)
            group_map(GROUPS - 1)
            pe.wait_ge(s_yev, GROUPS)

            def with_means(r, n, b, col):
                begin(n)
                product(None, b, range(0, 2))
                pe.wait_ge(s_sq, r + 1)
                pe.wait_ge(s_msread, r + 1)
                means(headavg, hn[1 - b], 4)
                product(None, b, range(2, 5))
                ada_cols(2 * r + 8, col)
                product(None, b, range(5, KT)).then_inc(s_tile, 1)
                ada_cols(2 * r + 9, col + 2)

            with pe.Fori(0, NPAIR) as j:
                with_means(2 * j, 2 * j + (T_Q + 1), 1, 8 * j + 16)
                with_means(2 * j + 1, 2 * j + (T_Q + 2), 0, 8 * j + 20)
            pe.wait_ge(s_msread, 1 + 2 * NPAIR)

            def turn_v(q):
                pe.wait_ge(s_free, T_V + q + 1)
                if q:
                    pe.wait_ge(s_v, q)
                for j in range(SB):
                    mm = t_.transpose(ps[:, 4 + j // 4, P * (j % 4):P * (j % 4) + P], hn[q % 2][:, P * j:P * j + P],
                                      ident)
                mm.then_inc(s_vps, 1)

            for q in range(1, NPAIR + 1):
                if q < NPAIR:
                    begin(T_V + q)
                    product(None, q % 2, range(0, 3))
                turn_v(q - 1)
                if q < NPAIR:
                    product(None, q % 2, range(3, KT)).then_inc(s_tile, 1)
            pe.wait_ge(s_pcol, 4)

            with pe.Fori(0, NPAIR // 2) as it:
                def scores(n):
                    par, h, i = BODY[n]
                    b = n // NU
                    if n % NU == 0:
                        pe.wait_ge(s_pair, 2 * it + (b + 1))
                        pe.wait_ge(s_pairk, 2 * it + (b + 1))
                    if n >= 6:
                        pe.wait_ge(s_a, it * NB + n - 5)
                    rows = slice(64 * par, 64 * par + 64)
                    cols = slice(col0(n), HALF)
                    qcols = slice(HALF * h + col0(n), HALF * h + HALF)
                    keys = slice(P * i, P * i + P)
                    z = ps[:, n % 6, cols]
                    diagonal = P * i >= HALF * h
                    t_.matmul(z, kh[b][rows, keys], qh[b][rows, qcols], start=True, stop=False)
                    t_.matmul(z, kh[b][rows, keys], ql[b][rows, qcols], start=False, stop=False)
                    mm = t_.matmul(z, kl[b][rows, keys], qh[b][rows, qcols], start=False, stop=True)
                    if diagonal:
                        mm = t_.matmul(ps[:, n % 6, col0(n):col0(n) + P], ident_b[:, :], mask_b[:, :],
                                       start=False, stop=True, skip_group_check=True)
                    mm.then_inc(s_z, 1)

                def exponents(n):
                    par, h, i = BODY[n]
                    cols = slice(col0(n), HALF)
                    pe.wait_ge(s_llo[n % 2], it * (NB // 2) + n // 2 + 1)
                    t_.matmul(ps[:, n % 6, cols], tri[:, :], loss_hi[n % 4][:, cols], start=False, stop=False,
                              skip_group_check=True)
                    mm = t_.matmul(ps[:, n % 6, cols], tri[:, :], loss_lo[n % 4][:, cols], start=False, stop=True,
                                   skip_group_check=True)
                    if i != 4 * h + 3:
                        pe.wait_ge(s_r, it * ADDS_BEFORE[NB] + ADDS_BEFORE[n])
                        cols = slice(col0(n - 1), HALF)
                        mm = t_.matmul(ps[:, n % 6, cols], ones[:, :], later[n % 2][:, cols], start=False, stop=True,
                                       skip_group_check=True)
                    mm.then_inc(s_e, 1)

                def outputs(n):
                    par, h, i = BODY[n]
                    b, s = n // NU, SEQ_OF[n]
                    cols = slice(col0(n), HALF)
                    if n % NU == 0:
                        pe.wait_ge(s_vp, 2 * it + (b + 1))
                    if i == 4 * h + 3 and s >= 2:
                        pe.wait_ge(s_ofree, it * NSEQ + s - 1)
                    pe.wait_ge(s_a, it * NB + n + 1)
                    mm = t_.matmul(ps[64 * par:64 * par + 64, 6 + s % 2, cols], vp[b][:, i, 64 * par:64 * par + 64],
                                   attn[n % 4][:, cols], start=(i == 4 * h + 3), stop=(i == 0), skip_group_check=True)
                    mm.then_inc(s_av, 1)

                for n in range(NB + 5):
                    if n < NB:
                        scores(n)
                    if 4 <= n < NB + 4:
                        exponents(n - 4)
                    if n >= 5:
                        outputs(n - 5)

            def out_means(p):
                pe.wait_ge(s_osq, p + 1)
                if p >= 2:
                    pe.wait_ge(s_msread, 2 * NPAIR + p)
                means(headavg, osq[p], 4 + 2 * (p % 2))

            begin(T_OUT)
            pe.wait_ge(s_mix, 2)
            pe.wait_ge(s_mixv, 2)
            product(0, 0, range(0, 2))
            out_means(0)
            out_means(1)
            begin(T_OUT + 1)
            product(1, 1, range(0, 2))
            product(0, 0, range(2, 4))
            out_means(2)
            product(1, 1, range(2, 4))
            out_means(3)
            two_tiles(range(4, KT), lambda k: (s_mixv, k - 1))
            with pe.Fori(1, KT // 2) as j:
                tile(2 * j + T_OUT, 0)
                tile(2 * j + (T_OUT + 1), 1)
            pe.wait_ge(s_ssum, 2 * (KT - 1) + KT - 2)
            pe.wait_ge(s_msread, 1 + 3 * NPAIR)
            for h in range(2):
                t_.matmul(ps[:, 4 + h, :], ones[:, :], ssum[:, HALF * h:HALF * h + HALF], start=True, stop=False)
            pe.wait_ge(s_sq2, KT)
            for h in range(2):
                mm = t_.matmul(ps[:, 4 + h, :], ones[:, :], sq2[(KT - 1) % 2][:, HALF * h:HALF * h + HALF],
                               start=False, stop=True)
            mm.then_inc(s_ms, 1)

            def down(g, m, ks=range(2)):
                if m == 0 and 0 in ks:
                    pe.wait_ge(s_wds, g + 1)
                if 0 in ks and not (isinstance(g, int) and 8 * g + m < 2):
                    pe.wait_ge(s_dev, 8 * g + (m - 1))
                for k in ks:
                    if m == 0 and k == 1 and isinstance(g, int) and g == NG - 1:
                        pe.wait_ge(s_fflast, 1)
                    elif m == 0:
                        pe.wait_ge(s_ff, 2 * g + (k + 1))
                    seq = [(wd_hi, ff_hi, 0), (wd_hi, ff_hi, 1), (wd_hi, ff_lo, 0), (wd_hi, ff_lo, 1),
                           (wd_lo, ff_hi, 0), (wd_lo, ff_hi, 1)]
                    for j, (w, a, h) in enumerate(seq):
                        mm = t_.matmul(ps[:, 4 + 2 * (m % 2) + h, :], w[:, k, P * m:P * m + P],
                                       a[:, k, HALF * h:HALF * h + HALF], start=(k == 0 and j < 2),
                                       stop=(k == 1 and j >= 4))
                if 1 in ks:
                    mm.then_inc(s_down, 1)

            begin(T_UP)
            begin(T_UP + 1)
            two_tiles(range(KT), lambda k: (s_act, KT + k + 1))
            tile(T_UP + 2, 0, begin_up)
            tile(T_UP + 3, 1, begin_up)

            def up_and_down(g):
                tile(4 * g + T_UP, 0, begin_up)
                tile(4 * g + (T_UP + 1), 1, begin_up)
                for m in range(KT):
                    down(g - 1, m)
                tile(4 * g + (T_UP + 2), 0, begin_up)
                tile(4 * g + (T_UP + 3), 1, begin_up)

            up_and_down(1)
            with pe.Fori(2, NG) as g:
                up_and_down(g)
            down(NG - 1, 0, [0])
            down(NG - 1, 1, [0])
            down(NG - 1, 0, [1])
            for m in range(KT + 1):
                if m < KT:
                    if m:
                        down(NG - 1, m, [1] if m == 1 else [0, 1])
                if m:
                    q = m - 1
                    pe.wait_ge(s_dev, 8 * (NG - 1) + q + 1)
                    if q >= 2:
                        pe.wait_ge(s_oev, q - 1)
                    for j in range(SB):
                        mm = t_.transpose(ps[:, 2 * (q % 2) + j // 4, P * (j % 4):P * (j % 4) + P],
                                          xT[:, q, P * j:P * j + P], ident)
                    mm.then_inc(s_tout, 1)


_OUTS = [((1, 1024, 1024), 'float32')]
_INS = ['x', 'c', 'ada_w', 'ada_b', 'norm1_g', 'w_in', 'pool_w', 'pool_b', 'pool_scale', 'q_norm_g', 'k_norm_g',
        'attn_out_g', 'w_out', 'norm2_g', 'w_up', 'conv_w', 'conv_b', 'w_down']


def kernel(**inputs):
    import numpy as _np
    import concourse.bacc as _bacc
    from concourse import mybir as _mybir
    from concourse.bass_utils import run_bass_kernel_spmd as _run

    nc = _bacc.Bacc("TRN2", target_bir_lowering=False, num_devices=1)
    arrays, args = {}, []
    for name in _INS:
        a = _np.ascontiguousarray(inputs[name])
        arrays[f"in_{name}_dram"] = a
        args.append(nc.dram_tensor(f"in_{name}_dram", a.shape, _mybir.dt.from_np(a.dtype), kind="ExternalInput").ap())
    arrays["in_consts_dram"] = shape_constants()
    args.append(nc.dram_tensor("in_consts_dram", (P, C_END), F32, kind="ExternalInput").ap())
    for i, (shape, dtype) in enumerate(_OUTS):
        dt = _mybir.dt.from_np(_np.dtype(dtype))
        args.append(nc.dram_tensor(f"out_{i}_dram", shape, dt, kind="ExternalOutput").ap())
    hybrid_layer(nc, *args)
    r = _run(nc, [arrays], core_ids=[0])
    return r.results[0]["out_0_dram"]
```
